# Optimizing a Trainium2 kernel written in Bass

```python
import math
import jax, jax.numpy as jnp
from jax import lax
import numpy as np

D_MODEL = 1024
BATCH = 1
SEQ = 512
DEPTH = 1

GRID_W = 64
CTX_LEN = 256
N_DA_HEADS = 4
DA_HEAD_DIM = 64
DA_V_DIM = 2 * DA_HEAD_DIM
QK_WIDTH = N_DA_HEADS * 2 * DA_HEAD_DIM
ATTN_WIDTH = N_DA_HEADS * DA_V_DIM
N_FOURIER_GROUPS = 4
FOURIER_GROUP_DIM = 128
FOURIER_WIDTH = N_FOURIER_GROUPS * FOURIER_GROUP_DIM
MIX_WIDTH = ATTN_WIDTH + FOURIER_WIDTH
IN_PROJ_WIDTH = 2 * QK_WIDTH + ATTN_WIDTH + FOURIER_WIDTH
ROPE_THETA = 10000.0
ROPE_AXIS_DIM = DA_HEAD_DIM // 2
Q_BLOCK = 128
N_GROUPS = 4
EXPERTS_PER_GROUP = 8
N_EXPERTS = N_GROUPS * EXPERTS_PER_GROUP
TOP_K = 2
D_EXPERT = 512
MOE_BLOCK = 128
N_MOD = 6
EPS = 1e-6


def rms_norm(x, g):
    xf = x.astype(jnp.float32)
    y = xf * lax.rsqrt(jnp.mean(xf * xf, axis=-1, keepdims=True) + EPS)
    return (y * g.astype(jnp.float32)).astype(x.dtype)

def modulate(h, shift, scale):
    return h * (1 + scale) + shift

def axial_rope_tables(rows, dtype):
    r, col = jnp.meshgrid(jnp.arange(rows), jnp.arange(GRID_W), indexing='ij')
    pos = jnp.stack([r.reshape(-1), col.reshape(-1)], axis=-1).astype(jnp.float32)
    inv_freq = ROPE_THETA ** (-jnp.arange(0, ROPE_AXIS_DIM, 2, dtype=jnp.float32) / ROPE_AXIS_DIM)
    ang = pos[:, :, None] * inv_freq
    ang = jnp.concatenate([ang, ang], axis=-1)
    return jnp.cos(ang).astype(dtype), jnp.sin(ang).astype(dtype)

def apply_axial_rope(x, cos, sin):
    xr = x.reshape(*x.shape[:-1], 2, ROPE_AXIS_DIM)
    x1, x2 = jnp.split(xr, 2, axis=-1)
    rot = jnp.concatenate([-x2, x1], axis=-1)
    c = cos[None, :, None, None]
    s = sin[None, :, None, None]
    return (xr * c + rot * s).reshape(x.shape)

def diff_lambda(lq1, lk1, lq2, lk2, lambda_init):
    f = lambda a: a.astype(jnp.float32)
    return jnp.exp(jnp.sum(f(lq1) * f(lk1))) - jnp.exp(jnp.sum(f(lq2) * f(lk2))) + lambda_init

def diff_attention(q, k, v, lam, g_subln, lambda_init):
    b, n = q.shape[:2]
    nb = n // Q_BLOCK
    qb = jnp.moveaxis(q.reshape(b, nb, Q_BLOCK, *q.shape[2:]), 1, 0)
    scale = DA_HEAD_DIM ** -0.5

    def block(qi):
        s = jnp.einsum('bqhmd,bkhmd->bhmqk', qi, k, preferred_element_type=jnp.float32) * scale
        p = jax.nn.softmax(s, axis=-1)
        a = p[:, :, 0] - lam * p[:, :, 1]
        return jnp.einsum('bhqk,bkhv->bqhv', a.astype(v.dtype), v)

    o = lax.map(block, qb)
    o = jnp.moveaxis(o, 0, 1).reshape(b, n, N_DA_HEADS, DA_V_DIM)
    o = rms_norm(o, g_subln) * (1.0 - lambda_init)
    return o.reshape(b, n, ATTN_WIDTH)

def fourier_mix(f, w_fourier):
    b, n, _ = f.shape
    fg = f.reshape(b, n, N_FOURIER_GROUPS, FOURIER_GROUP_DIM).astype(jnp.float32)
    fr = jnp.fft.fft2(fg, axes=(1, 3), norm='ortho').real.astype(f.dtype)
    return jnp.einsum('bngc,gcd->bngd', fr, w_fourier).reshape(b, n, FOURIER_WIDTH)

def hier_moe(h, w_rg, b_rg, w_re, b_re, w_gate, w_up, w_down):
    t, d = h.shape
    hf = h.astype(jnp.float32)
    g_logits = hf @ w_rg.astype(jnp.float32) + b_rg.astype(jnp.float32)
    grp = jnp.argmax(g_logits, axis=-1)
    p_grp = jnp.take_along_axis(jax.nn.softmax(g_logits, axis=-1), grp[:, None], axis=-1)
    e_logits = (hf @ w_re.astype(jnp.float32) + b_re.astype(jnp.float32)).reshape(t, N_GROUPS, EXPERTS_PER_GROUP)
    e_in = jnp.take_along_axis(e_logits, grp[:, None, None], axis=1)[:, 0]
    top_val, top_idx = lax.top_k(e_in, TOP_K)
    gate = p_grp * jax.nn.softmax(top_val, axis=-1)
    expert = grp[:, None] * EXPERTS_PER_GROUP + top_idx

    n_assign = t * TOP_K
    e_flat = expert.reshape(n_assign).astype(jnp.int32)
    tok_flat = jnp.repeat(jnp.arange(t, dtype=jnp.int32), TOP_K)
    w_flat = gate.reshape(n_assign)
    order = jnp.argsort(e_flat)
    e_sorted = e_flat[order]
    counts = jnp.bincount(e_flat, length=N_EXPERTS).astype(jnp.int32)
    starts = jnp.cumsum(counts) - counts
    padded = (counts + MOE_BLOCK - 1) // MOE_BLOCK * MOE_BLOCK
    pad_ends = jnp.cumsum(padded)
    pad_starts = pad_ends - padded
    dest = pad_starts[e_sorted] + jnp.arange(n_assign, dtype=jnp.int32) - starts[e_sorted]
    n_blocks = -(-n_assign // MOE_BLOCK) + N_EXPERTS
    buf_tok = jnp.full((n_blocks * MOE_BLOCK,), t, jnp.int32).at[dest].set(tok_flat[order])
    buf_w = jnp.zeros((n_blocks * MOE_BLOCK,), h.dtype).at[dest].set(w_flat[order].astype(h.dtype))
    block_expert = jnp.minimum(
        jnp.searchsorted(pad_ends, jnp.arange(n_blocks, dtype=jnp.int32) * MOE_BLOCK, side='right'),
        N_EXPERTS - 1)
    h_pad = jnp.concatenate([h, jnp.zeros((1, d), h.dtype)], axis=0)

    def expert_block(args):
        tok, wt, e = args
        xb = h_pad[tok]
        y = (jax.nn.silu(xb @ w_gate[e]) * (xb @ w_up[e])) @ w_down[e]
        return y * wt[:, None]

    ys = lax.map(expert_block, (buf_tok.reshape(n_blocks, MOE_BLOCK),
                                buf_w.reshape(n_blocks, MOE_BLOCK), block_expert))
    out = jnp.zeros((t + 1, d), ys.dtype).at[buf_tok].add(ys.reshape(-1, d))
    return out[:t]

def first_inputs(seed: int = 0) -> dict:
    key = jax.random.key(seed)
    ks = jax.random.split(key, 24)
    f32 = jnp.float32
    nrm = lambda k, shape, std: jax.random.normal(k, shape, f32) * std
    L = DEPTH
    return {
        'x': nrm(ks[0], (BATCH, SEQ, D_MODEL), 1.0),
        'c': nrm(ks[1], (BATCH, D_MODEL), 1.0),
        'ctx': nrm(ks[2], (BATCH, CTX_LEN, D_MODEL), 1.0),
        'c_ctx': nrm(ks[3], (D_MODEL,), 1.0),
        'w_ada': nrm(ks[4], (L, D_MODEL, N_MOD * D_MODEL), 0.5 * D_MODEL ** -0.5),
        'b_ada': nrm(ks[5], (L, N_MOD * D_MODEL), 0.02),
        'g_mix_norm': 1.0 + nrm(ks[6], (L, D_MODEL), 0.02),
        'g_ffn_norm': 1.0 + nrm(ks[7], (L, D_MODEL), 0.02),
        'w_in': nrm(ks[8], (L, D_MODEL, IN_PROJ_WIDTH), D_MODEL ** -0.5),
        'lambda_q1': nrm(ks[9], (L, DA_HEAD_DIM), 0.1),
        'lambda_k1': nrm(ks[10], (L, DA_HEAD_DIM), 0.1),
        'lambda_q2': nrm(ks[11], (L, DA_HEAD_DIM), 0.1),
        'lambda_k2': nrm(ks[12], (L, DA_HEAD_DIM), 0.1),
        'g_subln': 1.0 + nrm(ks[13], (L, DA_V_DIM), 0.02),
        'w_fourier': nrm(ks[14], (L, N_FOURIER_GROUPS, FOURIER_GROUP_DIM, FOURIER_GROUP_DIM), FOURIER_GROUP_DIM ** -0.5),
        'w_out': nrm(ks[15], (L, MIX_WIDTH, D_MODEL), MIX_WIDTH ** -0.5),
        'w_router_group': nrm(ks[16], (L, D_MODEL, N_GROUPS), D_MODEL ** -0.5),
        'b_router_group': nrm(ks[17], (L, N_GROUPS), 0.01),
        'w_router_expert': nrm(ks[18], (L, D_MODEL, N_EXPERTS), D_MODEL ** -0.5),
        'b_router_expert': nrm(ks[19], (L, N_EXPERTS), 0.01),
        'w_gate': nrm(ks[20], (L, N_EXPERTS, D_MODEL, D_EXPERT), D_MODEL ** -0.5),
        'w_up': nrm(ks[21], (L, N_EXPERTS, D_MODEL, D_EXPERT), D_MODEL ** -0.5),
        'w_down': nrm(ks[22], (L, N_EXPERTS, D_EXPERT, D_MODEL), D_EXPERT ** -0.5),
        'g_final': 1.0 + nrm(ks[23], (D_MODEL,), 0.02),
    }

def first_block(x, c, ctx, c_ctx, w_ada, b_ada, g_mix_norm, g_ffn_norm, w_in,
              lambda_q1, lambda_k1, lambda_q2, lambda_k2, g_subln, w_fourier, w_out,
              w_router_group, b_router_group, w_router_expert, b_router_expert,
              w_gate, w_up, w_down, g_final):
    b, s, d = x.shape
    n_ctx = ctx.shape[1]
    ROWS = s // GRID_W
    cos, sin = axial_rope_tables(ROWS, x.dtype)
    o_k = QK_WIDTH
    o_v = 2 * QK_WIDTH
    o_f = 2 * QK_WIDTH + ATTN_WIDTH
    xl, xc = x, ctx
    for l in range(DEPTH):
        last = l == DEPTH - 1
        lambda_init = 0.8 - 0.6 * math.exp(-0.3 * l)
        lam = diff_lambda(lambda_q1[l], lambda_k1[l], lambda_q2[l], lambda_k2[l], lambda_init)
        mod_l = (jax.nn.silu(c) @ w_ada[l] + b_ada[l]).reshape(b, N_MOD, 1, d)
        mod_c = (jax.nn.silu(c_ctx) @ w_ada[l] + b_ada[l]).reshape(N_MOD, d)
        sh1, sc1, gt1, sh2, sc2, gt2 = (mod_l[:, i] for i in range(N_MOD))
        csh1, csc1, cgt1, csh2, csc2, cgt2 = (mod_c[i] for i in range(N_MOD))
        wl = w_in[l]
        moe_args = (w_router_group[l], b_router_group[l], w_router_expert[l], b_router_expert[l],
                    w_gate[l], w_up[l], w_down[l])

        hl = modulate(rms_norm(xl, g_mix_norm[l]), sh1, sc1)
        pl = hl @ wl
        ql = apply_axial_rope(pl[..., :o_k].reshape(b, s, N_DA_HEADS, 2, DA_HEAD_DIM), cos, sin)
        kl = apply_axial_rope(pl[..., o_k:o_v].reshape(b, s, N_DA_HEADS, 2, DA_HEAD_DIM), cos, sin)
        vl = pl[..., o_v:o_f].reshape(b, s, N_DA_HEADS, DA_V_DIM)
        fl = pl[..., o_f:]

        hc = modulate(rms_norm(xc, g_mix_norm[l]), csh1, csc1)
        pc_kv = hc @ wl[:, o_k:o_f]
        kc = pc_kv[..., :QK_WIDTH].reshape(b, n_ctx, N_DA_HEADS, 2, DA_HEAD_DIM)
        vc = pc_kv[..., QK_WIDTH:].reshape(b, n_ctx, N_DA_HEADS, DA_V_DIM)

        k_all = jnp.concatenate([kc, kl], axis=1)
        v_all = jnp.concatenate([vc, vl], axis=1)
        mix_l = jnp.concatenate([diff_attention(ql, k_all, v_all, lam, g_subln[l], lambda_init),
                                 fourier_mix(fl, w_fourier[l])], axis=-1)
        xl = xl + gt1 * (mix_l @ w_out[l])
        h2l = modulate(rms_norm(xl, g_ffn_norm[l]), sh2, sc2)

        if last:
            xl = xl + gt2 * hier_moe(h2l.reshape(b * s, d), *moe_args).reshape(b, s, d)
        else:
            qc = (hc @ wl[:, :o_k]).reshape(b, n_ctx, N_DA_HEADS, 2, DA_HEAD_DIM)
            fc = hc @ wl[:, o_f:]
            mix_c = jnp.concatenate([diff_attention(qc, kc, vc, lam, g_subln[l], lambda_init),
                                     fourier_mix(fc, w_fourier[l])], axis=-1)
            xc = xc + cgt1 * (mix_c @ w_out[l])
            h2c = modulate(rms_norm(xc, g_ffn_norm[l]), csh2, csc2)
            y = hier_moe(jnp.concatenate([h2l.reshape(b * s, d), h2c.reshape(b * n_ctx, d)], axis=0), *moe_args)
            xl = xl + gt2 * y[:b * s].reshape(b, s, d)
            xc = xc + cgt2 * y[b * s:].reshape(b, n_ctx, d)
    return rms_norm(xl, g_final)


SB_HEADS = 8
SB_HEAD_DIM = 64
SB_WIDTH = SB_HEADS * SB_HEAD_DIM
SB_BLOCK = 128

GDN_HEADS = 4
GDN_HEAD_DIM = 128
GDN_WIDTH = GDN_HEADS * GDN_HEAD_DIM
GDN_CHUNK = 64
CONV_K = 4


SPLIT_SIZES = (3 * SB_WIDTH, SB_WIDTH, 3 * GDN_WIDTH, GDN_WIDTH, GDN_HEADS, GDN_HEADS, D_MODEL, D_MODEL)
N_IN = 3 * SB_WIDTH + SB_WIDTH + 3 * GDN_WIDTH + GDN_WIDTH + 2 * GDN_HEADS + 2 * D_MODEL


def rms_norm_2(x, w):
    xf = x.astype(jnp.float32)
    y = xf * lax.rsqrt(jnp.mean(xf * xf, axis=-1, keepdims=True) + EPS)
    return (y * w.astype(jnp.float32)).astype(x.dtype)

def l2_normalize(x):
    return x * lax.rsqrt(jnp.sum(x * x, axis=-1, keepdims=True) + EPS)

def split_heads(t, n_heads, head_dim):
    b, s, _ = t.shape
    return t.reshape(b, s, n_heads, head_dim).transpose(0, 2, 1, 3)

def merge_heads(t):
    b, h, s, d = t.shape
    return t.transpose(0, 2, 1, 3).reshape(b, s, h * d)

def stick_breaking_attention(q, k, v):
    seq = q.shape[2]
    scale = SB_HEAD_DIM ** -0.5
    outs = []
    for blk in range(seq // SB_BLOCK):
        t0 = blk * SB_BLOCK
        t1 = t0 + SB_BLOCK
        qb = q[:, :, t0:t1].astype(jnp.float32)
        kb = k[:, :, :t1].astype(jnp.float32)
        vb = v[:, :, :t1].astype(jnp.float32)
        z = jnp.einsum('bhqd,bhkd->bhqk', qb, kb) * scale
        q_pos = t0 + jnp.arange(SB_BLOCK)[:, None]
        k_pos = jnp.arange(t1)[None, :]
        causal = k_pos < q_pos
        log_keep = jnp.where(causal, -jax.nn.softplus(z), 0.0)
        suffix = lax.cumsum(log_keep, axis=3, reverse=True) - log_keep
        log_a = jax.nn.log_sigmoid(z) + suffix
        a = jnp.where(causal, jnp.exp(log_a), 0.0)
        outs.append(jnp.einsum('bhqk,bhkd->bhqd', a, vb))
    return jnp.concatenate(outs, axis=2).astype(q.dtype)

def causal_depthwise_conv(x, w):
    channels = x.shape[-1]
    return lax.conv_general_dilated(
        x, w[:, None, :].astype(x.dtype), window_strides=(1,), padding=[(CONV_K - 1, 0)],
        dimension_numbers=('NWC', 'WIO', 'NWC'), feature_group_count=channels)

def gated_delta_rule_chunked(q, k, v, g, beta):
    b, h, seq, dk = q.shape
    dv = v.shape[-1]
    c = GDN_CHUNK
    n = seq // c
    q = q * dk ** -0.5
    q = q.reshape(b, h, n, c, dk)
    k = k.reshape(b, h, n, c, dk)
    v = v.reshape(b, h, n, c, dv)
    beta = beta.reshape(b, h, n, c)
    g = jnp.cumsum(g.reshape(b, h, n, c), axis=-1)
    idx = jnp.arange(c)
    lower_incl = idx[:, None] >= idx[None, :]
    strict = idx[:, None] > idx[None, :]
    decay = jnp.exp(jnp.where(lower_incl, g[..., :, None] - g[..., None, :], -jnp.inf))
    kk = jnp.einsum('bhnid,bhnjd->bhnij', k, k)
    m = jnp.where(strict, beta[..., :, None] * kk * decay, 0.0)
    rhs = jnp.concatenate([v * beta[..., None], k * (beta * jnp.exp(g))[..., None]], axis=-1)
    sol = lax.linalg.triangular_solve(m, rhs, left_side=True, lower=True, unit_diagonal=True)
    u = sol[..., :dv]
    w = sol[..., dv:]
    intra = jnp.where(lower_incl, jnp.einsum('bhnid,bhnjd->bhnij', q, k) * decay, 0.0)

    def step(state, inp):
        q_c, k_c, u_c, w_c, g_c, intra_c = inp
        v_new = u_c - jnp.einsum('bhcd,bhde->bhce', w_c, state)
        o = (jnp.einsum('bhcd,bhde->bhce', q_c * jnp.exp(g_c)[..., None], state)
             + jnp.einsum('bhij,bhje->bhie', intra_c, v_new))
        g_last = g_c[..., -1:]
        state = (state * jnp.exp(g_last)[..., None]
                 + jnp.einsum('bhcd,bhce->bhde', k_c * jnp.exp(g_last - g_c)[..., None], v_new))
        return state, o

    chunk_first = lambda t: jnp.moveaxis(t, 2, 0)
    xs = tuple(chunk_first(t) for t in (q, k, u, w, g, intra))
    state0 = jnp.zeros((b, h, dk, dv), jnp.float32)
    _, o = lax.scan(step, state0, xs)
    return jnp.moveaxis(o, 0, 2).reshape(b, h, seq, dv)

def hybrid_layer(x, pre_w, post_w, w_in, conv_w, a_log, dt_bias, gdn_norm_w,
                 w_branch_sb, w_branch_gdn, w_out):
    f32 = jnp.float32
    h = rms_norm_2(x, pre_w)
    proj = h @ w_in
    points = [int(p) for p in np.cumsum(SPLIT_SIZES)[:-1]]
    sb_qkv, sb_gate, gdn_qkv, gdn_gate, gdn_a, gdn_b, merge_sb, merge_gdn = jnp.split(proj, points, axis=-1)

    q_sb, k_sb, v_sb = [split_heads(t, SB_HEADS, SB_HEAD_DIM) for t in jnp.split(sb_qkv, 3, axis=-1)]
    o_sb = merge_heads(stick_breaking_attention(q_sb, k_sb, v_sb)) * jax.nn.silu(sb_gate)

    gdn_qkv = jax.nn.silu(causal_depthwise_conv(gdn_qkv, conv_w))
    q_g, k_g, v_g = [split_heads(t, GDN_HEADS, GDN_HEAD_DIM).astype(f32) for t in jnp.split(gdn_qkv, 3, axis=-1)]
    q_g = l2_normalize(q_g)
    k_g = l2_normalize(k_g)
    g = (-jnp.exp(a_log.astype(f32)) * jax.nn.softplus(gdn_a.astype(f32) + dt_bias.astype(f32))).transpose(0, 2, 1)
    beta = jax.nn.sigmoid(gdn_b.astype(f32)).transpose(0, 2, 1)
    o_g = gated_delta_rule_chunked(q_g, k_g, v_g, g, beta)
    o_g = merge_heads(rms_norm_2(o_g, gdn_norm_w)).astype(x.dtype) * jax.nn.silu(gdn_gate)

    merged = (jax.nn.sigmoid(merge_sb) * (o_sb @ w_branch_sb)
              + jax.nn.sigmoid(merge_gdn) * (o_g @ w_branch_gdn))
    y = merged @ w_out
    return x + rms_norm_2(y, post_w)

def second_inputs(seed: int = 0) -> dict:
    key = jax.random.key(seed)
    ks = jax.random.split(key, 12)
    f32 = jnp.float32

    def normal(k, shape, scale):
        return jax.random.normal(k, shape, f32) * scale

    x = normal(ks[0], (BATCH, SEQ, D_MODEL), 1.0)
    pre_norm_w = 1.0 + normal(ks[1], (DEPTH, D_MODEL), 0.05)
    post_norm_w = 1.0 + normal(ks[2], (DEPTH, D_MODEL), 0.05)
    w_in = normal(ks[3], (DEPTH, D_MODEL, N_IN), D_MODEL ** -0.5)
    conv_w = normal(ks[4], (DEPTH, CONV_K, 3 * GDN_WIDTH), CONV_K ** -0.5)
    a_log = jnp.log(jax.random.uniform(ks[5], (DEPTH, GDN_HEADS), f32, minval=0.5, maxval=16.0))
    dt = jnp.exp(jax.random.uniform(ks[6], (DEPTH, GDN_HEADS), f32,
                                    minval=math_log(0.001), maxval=math_log(0.1)))
    dt_bias = dt + jnp.log(-jnp.expm1(-dt))
    gdn_norm_w = 1.0 + normal(ks[7], (DEPTH, GDN_HEAD_DIM), 0.05)
    w_branch_sb = normal(ks[8], (DEPTH, SB_WIDTH, D_MODEL), SB_WIDTH ** -0.5)
    w_branch_gdn = normal(ks[9], (DEPTH, GDN_WIDTH, D_MODEL), GDN_WIDTH ** -0.5)
    w_out = normal(ks[10], (DEPTH, D_MODEL, D_MODEL), D_MODEL ** -0.5)
    return {"x": x, "pre_norm_w": pre_norm_w, "post_norm_w": post_norm_w, "w_in": w_in,
            "conv_w": conv_w, "a_log": a_log, "dt_bias": dt_bias, "gdn_norm_w": gdn_norm_w,
            "w_branch_sb": w_branch_sb, "w_branch_gdn": w_branch_gdn, "w_out": w_out}

def math_log(v):
    return float(np.log(v))

def second_block(x, pre_norm_w, post_norm_w, w_in, conv_w, a_log, dt_bias, gdn_norm_w,
              w_branch_sb, w_branch_gdn, w_out):
    for layer in range(DEPTH):
        x = hybrid_layer(x, pre_norm_w[layer], post_norm_w[layer], w_in[layer], conv_w[layer],
                         a_log[layer], dt_bias[layer], gdn_norm_w[layer],
                         w_branch_sb[layer], w_branch_gdn[layer], w_out[layer])
    return x


def setup_inputs(seed=0):
    out = dict(first_inputs(seed))
    for name, value in second_inputs(seed + 1).items():
        if name != "x":
            out[name + "_2"] = value
    return out


def reference(
    x, c, ctx, c_ctx, w_ada, b_ada, g_mix_norm, g_ffn_norm, w_in, lambda_q1, lambda_k1,
    lambda_q2, lambda_k2, g_subln, w_fourier, w_out, w_router_group, b_router_group,
    w_router_expert, b_router_expert, w_gate, w_up, w_down, g_final, pre_norm_w_2,
    post_norm_w_2, w_in_2, conv_w_2, a_log_2, dt_bias_2, gdn_norm_w_2, w_branch_sb_2,
    w_branch_gdn_2, w_out_2,
):
    x = first_block(
        x, c, ctx, c_ctx, w_ada, b_ada, g_mix_norm, g_ffn_norm, w_in, lambda_q1, lambda_k1,
        lambda_q2, lambda_k2, g_subln, w_fourier, w_out, w_router_group, b_router_group,
        w_router_expert, b_router_expert, w_gate, w_up, w_down, g_final,
    )
    return second_block(
        x, pre_norm_w_2, post_norm_w_2, w_in_2, conv_w_2, a_log_2, dt_bias_2, gdn_norm_w_2,
        w_branch_sb_2, w_branch_gdn_2, w_out_2,
    )


_drawn_inputs = setup_inputs


def setup_inputs(seed=0):
    import zlib

    import numpy as np

    out = dict(_drawn_inputs(seed))
    spreads = {}
    factors = {'g_mix_norm': 7.408,
     'g_ffn_norm': 3.528,
     'lambda_q1': 8.0,
     'lambda_k1': 8.0,
     'lambda_k2': 36.392,
     'g_subln': 8.0,
     'b_router_group': 8.0,
     'b_router_expert': 6.302}
    for name, (base, spread) in spreads.items():
        noise = np.random.default_rng([zlib.crc32(name.encode()), seed]).standard_normal(out[name].shape)
        drawn = base * np.exp(spread * noise) if base else spread * noise
        out[name] = __import__('jax').numpy.asarray(drawn.astype(out[name].dtype))
    for name, factor in factors.items():
        out[name] = (out[name] * factor).astype(out[name].dtype)
    return out
```

```python
import math
from contextlib import ExitStack

import concourse.bass as bass
from concourse import mybir
import numpy as np

F32 = mybir.dt.float32
I32 = mybir.dt.int32
U32 = mybir.dt.uint32
ALU = mybir.AluOpType
ACT = mybir.ActivationFunctionType
AX = mybir.AxisListType

P = 128
D = 1024
KD = D // P
S = 512
NT = S // P
CTX = 256
NC = CTX // P
NKEY = CTX + S
KT = NKEY // P
H = 4
HD = 64
EPS = 1e-6
NEXP, NGRP, EPG = 32, 4, 8
CAP = 64
ROUNDS = S // CAP
NO_TOKEN = 4096
RING = 6
BLK = 4096
HS = 8
GSS = (2, 3, 0)
CHUNK = 64
EXP_AND_LOG = 6
LAMBDA_INIT = 0.8 - 0.6 * math.exp(-0.3 * 0)

B_ADA0, B_F, B_V, B_Q, B_K = 0, 4, 5, 6, 7
B_ADA1, B_WOUT = 8, 16
B_MOE = 18
B_SECOND = B_MOE + 3 * NEXP
SECOND = ["q", "k", "v", "gate_s", "gk", "gv", "gq", "gate_g", "ms0", "w_branch_sb_2", "ms1", "mg0", "w_branch_gdn_2", "mg1"]
RING2 = 4
CLEARED = {"cs": 1, "qscale": 3, "qz": 5, "fill": 6, "xg": 9, "stage": 10, "wab": 11, "qs": 13, "state": 16}
BROADCAST = {"lambda": 1, "gt1": 3, "ffn": 11, "rbias": 12, "postb": 13}

def from_where(**counts):
    out, n = {}, 0
    for name, steps in counts.items():
        out[name] = n
        n += steps
    return out


RMS = from_where(rstd=1, orstd=H, rstd1=NT, rstd2=2 * NT, ors2=1, frs=NT)
SMALL_EXP = from_where(c_exp=1, lambda_exp=1, router_exp=2, alog_exp=1, dt_ln=1, beta_exp=1, egc=1)
TENSOR_STEP = from_where(mod_turned=1, wcs_mm=1, logits_turned=1, ranks_mm=1, stage_turned=1, ab_mm=1, rows_turned=1)
VECTOR_STEP = from_where(modr_zero=1, silu_c=1, normed=NT + NC, lambda_sums=2, gains=2, wcs=2, chosen=1, flag=1, slots=1, row_numbers=1, prew=1, rows_zero=1, dt_abs=1, to_last=1)

NORMS = [("final", 0), ("final", 1), ("second", 0), ("final", 2), ("second", 1), ("final", 3), ("second", 2), ("second", 3)]


def at_norm(kind, q):
    return NORMS.index((kind, q)) + 1


def count_steps(kinds):
    out = {}
    for pair in range(2):
        for lv, group in kinds:
            for p in range(2):
                for kind in group:
                    key = (kind, 2 * pair + p) + ((lv,) if lv else ())
                    out[key] = len(out) + 1
    return out


SOLVE_MM = count_steps([(0, ["grow", "kk"]), (0, ["brow", "qk"]), (0, ["k", "v"]), (0, ["u0"])]
                       + [(lv, g) for lv in range(1, 6) for g in (["y"], ["t", "u"] if lv < 5 else ["u"])]
                       + [(0, ["u", "w"])])
SOLVE_DVE = count_steps([(0, ["dec", "egl", "half"]), (0, ["mt", "intra", "qe", "u0"]), (0, ["krhs", "kdec", "vrhs"]), (0, ["t0"])]
                        + [(lv, ["t", "u"] if lv < 5 else ["u"]) for lv in range(1, 6)] + [(0, ["w"])])

STICK_PLAN = []
for _h in range(8):
    for _what in ("z", "suffix", "attend"):
        STICK_PLAN.append((_what, _h))
        if _what != "attend" or _h % 2 == 0:
            STICK_PLAN.append(("fill", sum(w == "fill" for w, _ in STICK_PLAN)))
MERGE_AT = {point: n for n, point in enumerate(
    [("norm", 0), ("norm", 3), ("norm", 6)] + [("solve", pair, n) for pair in range(2) for n in range(4)] + [("chunk", c) for c in range(8)])}
COLS2 = {"q": 0, "k": 512, "v": 1024, "gate_s": 1536, "gq": 2048, "gk": 2560, "gv": 3072,
         "gate_g": 3584, "ab": 4096, "ms0": 4104, "ms1": 4616, "mg0": 5128, "mg1": 5640}


def constants():
    f = np.float32
    out = {}
    row, col = np.meshgrid(np.arange(S // 64), np.arange(64), indexing="ij")
    pos = np.stack([row.reshape(-1), col.reshape(-1)], -1).astype(f)
    inv = (f(10000.0) ** (-np.arange(0, 32, 2, dtype=f) / f(32))).astype(f)
    ang = (pos[:, :, None] * inv).astype(f)
    ang = np.concatenate([ang, ang], -1).reshape(S, HD)
    two = np.concatenate([ang, ang], -1).T
    out["rope"] = np.ascontiguousarray(np.stack([np.cos(two), np.sin(two)], 1)).astype(f)
    rot = np.zeros((P, P), f)
    for m in range(P):
        b, r = m // 32 * 32, m % 32
        rot[b + (r + 16) % 32, m] = -1.0 if r < 16 else 1.0
    n = np.arange(S)
    w = 2 * np.pi * (np.outer(n, n) % S) / S
    norm = 1.0 / math.sqrt(S * P)
    seq = np.stack([np.cos(w) * norm, -np.sin(w) * norm], 0).astype(f)
    out["dft_seq"] = np.ascontiguousarray(seq.reshape(2, NT, P, S).transpose(2, 0, 1, 3))
    c = np.arange(P)
    w = 2 * np.pi * (np.outer(c, c) % P) / P
    i, j = np.meshgrid(np.arange(P), np.arange(P), indexing="ij")
    sq = {
        "ident": np.eye(P), "ones": np.ones((P, P)), "rot": rot, "cos": np.cos(w), "sin": np.sin(w),
        "before": (i < j), "neg_from": -1.0 * (i >= j), "neg_ones": -np.ones((P, P)),
        "causal": (i <= j) & (i // CHUNK == j // CHUNK),
    }
    for lv in range(6):
        b = 1 << lv
        sq[f"join{lv}"] = (j // (2 * b) == i // (2 * b)) & (j // b % 2 == 1) & (i // b % 2 == 0)
    out["squares"] = np.ascontiguousarray(np.stack([v.astype(f) for v in sq.values()], 1))
    r = np.zeros((P, 8, NEXP), f)
    r[:, 0, :] = np.arange(NEXP)
    r[:, 1, :NGRP] = np.arange(NGRP)
    for k in range(2):
        for q in range(NT):
            r[:, 2, k * NT + q] = 2 * (q * P + np.arange(P)) + k
    r[:, 3, 0] = (np.arange(P) // CAP).astype(np.int32).view(f)
    out["router"] = r
    out["names"] = list(sq)
    return out


SQUARES = constants()["names"]


def program(nc, a, t, out, scratch):
    ctx = ExitStack()
    made = {}

    def sem(name):
        if name not in made:
            made[name] = ctx.enter_context(nc.semaphore(name))
        return made[name]

    with ctx:
        ring = ctx.enter_context(nc.sbuf_tensor("ring", [P, RING, BLK], F32))
        arena = ctx.enter_context(nc.sbuf_tensor("arena", [P, 28560], F32))
        ps = ctx.enter_context(nc.psum_tensor("ps", [P, 8, 512], F32))

        def at(word, *shape):
            n = math.prod(shape)
            v = arena[:, word:word + n]
            if len(shape) == 1:
                return v
            names = "abcd"[:len(shape)]
            return v.rearrange(f"p ({' '.join(names)}) -> p {' '.join(names)}",
                               **{x: n_ for x, n_ in zip(names[1:], shape[1:])})

        def bank(b, n=512):
            return ps[:, b, 0:n]

        def banks(b, n):
            return ps[:, b:b + -(-n // 512), :].rearrange("p a b -> p (a b)")[:, 0:n]

        def block(n):
            return ring[:, n % RING, :].rearrange("p (k n) -> p k n", k=KD)

        def block4(n):
            return ring[:, n % RING, :].rearrange("p (k n) -> p k n", k=4)

        dft_seq = at(0, 2, NT, S)
        x1 = at(0, NT, D)
        xc = at(4096, NT + NC, D)
        fT = at(4096, H, S)
        fcs = at(6144, NT, H, 2 * P)
        qz = at(4096, H, 2, S)
        kT = at(8192, H, NKEY)
        hT = at(11264, KD, S)
        hcT = at(15360, KD, CTX)
        mix_att = at(11264, H, S)
        prT = at(13312, KT, P)
        ex = at(14080, 2, 2, NKEY)
        oh = at(17152, 256)
        qraw = at(17408, 2, S)
        qcos = at(18432, S)
        gt1b = at(17408, D)
        v = at(18944, KT, S)
        wf = at(18944, H * P)
        wcs = at(19456, H, 2, P)
        mix_fou = at(22016, H, S)
        lamv = at(22016, 4, HD)
        lamb = at(22272, 4, HD)
        lamp = at(22528, 4, HD)
        modr = at(24064, 3, 512)
        rope = at(25600, 2, S)
        sq = at(26624, 6, P)
        IDENT, ONES, ROT, COS, SIN, BEFORE = (sq[:, n, :] for n in range(6))
        cs = at(27392, KD, 32)
        modc = at(27648, 4, P)
        small = at(28160, 400)

        def col(n, w=1):
            return small[:, n:n + w]

        c2 = col(0, 16).rearrange("p (m k) -> p m k", m=2)
        ce = col(16, 16)
        cden = col(32, 16)
        gain = col(48, 16).rearrange("p (m k) -> p m k", m=2)
        eps = col(64)
        ss = col(66, 6)
        lnss = col(72, 6)
        rstd = col(78, 6)
        nmax = col(84, 2)
        zsum = col(110, 4)
        rz = col(88, 2)
        lam = col(90)
        lams = col(92, 2)
        lame = col(94, 2)
        oss = col(96, 4)
        oln = col(100, 4)
        orstd = col(104, 4)
        gsub = col(108)
        gsub8 = col(109)
        mhc = modc.rearrange("p q (j m) -> p j q m", j=4)

        h2 = at(4096, NT, D)
        h2T = at(11264, KD, S)
        gsb = at(15360, D)
        sh2b = at(16384, D)
        gt2b = at(17408 + 1024, D)
        gfb = at(19456, D)
        gt2s = at(17664, 512)
        wr = at(20480, KD, 36)
        rbias = at(20768, 36)
        lgT = at(20808, S)
        rt = at(21320, 2700)
        gffb = at(10240, D)
        rowt = at(8192, 2, D)
        rcon = at(24064, 8, NEXP)
        tabs = at(24320, 3, ROUNDS * NEXP).bitcast(I32)

        def rv(word, *shape):
            n = math.prod(shape)
            return rt[:, word:word + n].rearrange("p (a b) -> p a b", b=shape[-1]) if len(shape) > 1 else rt[:, word:word + n]

        L = rv(0, NT, 36)
        cg = rv(144, NT, 4)
        ogr = rv(160, NT, 4)
        dg = rv(176, NT, 4)
        pen = rv(192, NT, 4)
        gm, gi, gs, m1, m2, i1, i2 = (rv(208 + 4 * n, NT) for n in range(7))
        d2, den2, r2, pg, pos = (rv(236 + 4 * n, NT) for n in range(5))
        wgt = col(120, 2 * NT).rearrange("p (k q) -> p k q", k=2)
        Em = rv(256, NT, NEXP)
        Ec = rv(384, NT, NEXP)
        O1 = rv(512, NT, NEXP)
        O2 = rv(640, NT, NEXP)
        As = rv(768, NT, NEXP)
        pre = rv(896, NT + 1, NEXP)
        Rk = rv(1056, NT, NEXP)
        tmpR = rv(1184, NT, NEXP)
        rk = rv(1312, 2, NT)
        ek = rv(1320, 2, NT)
        rki = rv(1328, 2 * NT).bitcast(I32)
        eki = rv(1336, 2 * NT).bitcast(I32)
        lo = rv(1344, 2 * NT).bitcast(I32)
        hi = rv(1352, 2 * NT).bitcast(I32)
        slot = rv(1360, 2 * NT).bitcast(I32)
        cnt = rv(1376, NEXP)
        val = rv(1408, 2 * NT).bitcast(I32)
        fill = ROT.bitcast(I32)
        flagf = col(130)
        flag = col(131).bitcast(I32)
        xg = at(4096, 2, 512)
        xeT = at(5120, 2, 4, P)
        he = at(6144, 2, 256)
        ge = at(6656, 4, 256)
        heT = at(7680, 2, P)
        ye = at(8192, 2, 512)
        ixr = at(9216, 2, 1).bitcast(U32)
        ixw = at(9220, 2, 1).bitcast(U32)
        ygo = at(9472, NT, 2, D)

        e0 = ring[:, 4, :]
        e1 = ring[:, 5, :]
        h3 = e0.rearrange("p (q n) -> p q n", q=NT)
        h3T = at(4096, KD, S)
        gdn = [at(8192 + 2048 * n, H, S) for n in range(3)]
        gk, gv, gq = gdn
        intra = at(14336, H, NT, P)
        wT = at(16384, H, NT, P)
        qs = at(18432, HS, S)
        ks = at(22528, H, S)
        vs = at(24576, NT, S)
        osb = e0[:, 0:2048].rearrange("p (c n) -> p c n", c=4)
        gg = e0[:, 2048:4096].rearrange("p (q n) -> p q n", q=NT)
        spz = [e1[:, o:o + S - kb * P] for kb, o in enumerate((0, 512, 896, 1152))]
        azz = [e1[:, 1280 + o:1280 + o + S - kb * P] for kb, o in enumerate((0, 512, 896, 1152))]
        ezz = [e1[:, 2560 + o:2560 + o + S - kb * P] for kb, o in enumerate((0, 512, 896, 1152))]
        sq2 = at(26880, 9, P)
        NEG_FROM, NEG_ONES, CAUSAL = (sq2[:, n, :] for n in range(3))
        JOIN = [sq2[:, 3 + n, :] for n in range(6)]
        cv = at(14336, 2, S)
        cu = at(15360, 2, S)
        wab = at(16384, KD, 64)
        rhs = at(18432, 2, NT, 2 * P)
        MT, Tm, Um, Mo, Yl = (at(20480 + 1024 * n, 2, NT, P) for n in range(5))
        dec = at(25600, 2, NT, P)
        rows = at(17920, S)
        keep = e0[:, 2048:2560]
        trow = e0[:, 2560:3072]
        trow2 = e0[:, 3072:3584]
        egrow = e1[:, 3072:4096].rearrange("p (a n) -> p a n", a=2)
        colsab = col(300, 48).rearrange("p (q c h) -> p q c h", q=NT, c=3)
        bg = col(348, 16).rearrange("p (q h) -> p q h", q=NT)
        egc = col(364, 16).rearrange("p (q h) -> p q h", q=NT)
        egl = at(28032, H, S // CHUNK)
        state = at(20480, 2, H, P)
        vE = at(21504, S)
        vO = at(22016, S)
        og = at(22528, NT, S)
        ogs = at(18432, S)
        ogT = at(24576, H, S)
        merged = e1.rearrange("p (k n) -> p k n", k=KD)
        sig = at(12288, 2, 2, S)
        junk = at(12288, D)
        yb = at(16384, NT, D)
        postb = at(22528, D)
        prow = at(23552, D)
        stage = at(28032, P)
        oss2 = col(140, 16)
        oln2 = col(156, 16)
        ors2 = col(172, 16)
        convw = col(200, 48).rearrange("p (i c) -> p i c", i=4)
        prew = col(248, KD)
        dtb = col(260)
        alog = col(261)
        nea = col(262)
        gnw = col(263)
        qscale = col(264)
        fss = col(266, 4)
        fln = col(270, 4)
        frs = col(274, 4)
        ss3 = col(280, 4)
        ln3 = col(284, 4)
        tick = col(292)
        rs3 = col(288, 4)

        block_ = ctx.enter_context(nc.Block())

        def cols(w, at_, n=512, pk=False):
            way = "(p k) n -> p k n" if pk else "(k p) n -> p k n"
            return w[:, at_:at_ + n].rearrange(way, p=P)

        def before_moe():
            ada = a["w_ada"][0]
            win = a["w_in"][0]
            for j in range(4):
                yield cols(ada, 512 * j, pk=True)
            for c0 in (1536, 1024, 0, 512):
                yield cols(win, c0)
            for j in range(4, 12):
                yield cols(ada, 512 * j, pk=True)
            for j in range(2):
                yield cols(a["w_out"][0], 512 * j)

        def second_weights():
            for name in SECOND:
                if name in COLS2:
                    yield cols(a["w_in_2"][0], COLS2[name])
                else:
                    yield a[name][0].rearrange("(k p) n -> p k n", p=P)
            for j in range(2):
                yield cols(a["w_out_2"][0], 512 * j)

        def expert_weights(e):
            one = bass.ds(e, 1)
            return (a["w_gate"][0, one].rearrange("a (k p) n -> p (a k) n", p=P),
                    a["w_up"][0, one].rearrange("a (k p) n -> p (a k) n", p=P),
                    a["w_down"][0, one].rearrange("a (k p) n -> p (a k) n", p=P))

        def oz(q):
            return rope.rearrange("p a b -> p (a b)")[:, q * P:(q + 1) * P]

        act_count = [0]

        def act_link(act, ins):
            act_count[0] += 1
            ins.then_inc(sem("act_chain"), 1)
            act.wait_ge(sem("act_chain"), act_count[0])

        def act_norm(act, n):
            act.wait_ge(sem("gss_mm"), n + 1)
            if n >= 2:
                act.wait_ge(sem("gnormed"), n - 1)
            act_link(act, nc.scalar.activation(cv[:, n % 2, :], bank(GSS[n % 3]), ACT.Ln, bias=eps))
            if n < H:
                nc.scalar.activation(cv[:, n % 2, :], cv[:, n % 2, :], ACT.Exp, scale=-0.5).then_inc(sem("gexp"), 1)
            else:
                nc.scalar.activation(cv[:, n % 2, :], cv[:, n % 2, :], ACT.Exp, scale=-0.5, bias=qscale).then_inc(sem("gexp"), 1)

        def act_prT(act, i):
            act.wait_ge(sem("pr_turned"), i + 1)
            if i >= 1:
                act.wait_ge(sem("o_mm"), i)
            nc.scalar.copy(prT.rearrange("p a b -> p (a b)"), banks(4, NKEY)).then_inc(sem("prT"), 1)

        def act_subln(act, h):
            act.wait_ge(sem("o_mm"), NT * (h + 1))
            for q in range(NT):
                act_link(act, nc.scalar.activation(oh[:, 0:P], ps[:, 6, q * P:(q + 1) * P], ACT.Square,
                                     accum_out=oss[:, q:q + 1]))
            act_link(act, nc.scalar.activation(oln, oss, ACT.Ln, scale=1.0 / P, bias=eps))
            nc.scalar.activation(orstd, oln, ACT.Exp, scale=-0.5).then_inc(sem("rms"), 1)

        @block_.sync
        def _(sp):
            def load(n, src):
                if n >= RING:
                    sp.wait_ge(sem("blocks_used"), n - RING + 1)
                dst = block(n) if src.shape[1] == KD else block4(n)
                sp.dma_start(dst, src).then_inc(sem(f"block_in_{n % RING}"), 16)

            for n, src in enumerate(before_moe()):
                load(n, src)
            with sp.Fori(0, NEXP // 2) as i:
                for u in range(2):
                    for w, src in enumerate(expert_weights(2 * i + u)):
                        s_ = 3 * u + w
                        sp.wait_ge(sem("blocks_used"), 6 * i + (B_MOE - RING + 1 + s_))
                        dst = ring[:, s_, :].rearrange("p (k n) -> p k n", k=src.shape[1])
                        sp.dma_start(dst, src).then_inc(sem(f"block_in_{s_}"), 16)
            sp.wait_ge(sem("vector_step"), VECTOR_STEP["flag"] + 1)
            more = sp.value_load(flag[0:1, 0:1], min_val=0, max_val=1)
            with sp.If(more > 0):
                with sp.Fori(1, ROUNDS) as r:
                    with sp.Fori(0, NEXP) as e:
                        n = NEXP * r + e - NEXP
                        sp.wait_ge(sem("blocks_used"), B_SECOND)
                        sp.wait_ge(sem("more_done"), n + 1)
                        for w, src in enumerate(expert_weights(e)):
                            sp.dma_start(ring[:, w, :].rearrange("p (k n) -> p k n", k=src.shape[1]), src).then_inc(sem("more_in"), 16)
                sp.wait_ge(sem("more_done"), (ROUNDS - 1) * NEXP + 1)
            for m, src in enumerate(second_weights()):
                if m == 1:
                    for n in range(2):
                        sp.wait_ge(sem(f"y_in_{n}"), 32)
                sp.wait_ge(sem("blocks_used"), B_SECOND + m - (RING if m < RING2 else RING2) + 1)
                dst = ring[:, m % RING2, :].rearrange("p (k n) -> p k n", k=src.shape[1])
                sp.dma_start(dst, src).then_inc(sem(f"block_in_{m % RING2}"), 16)
            for q in range(NT):
                sp.wait_ge(sem("out_ready"), q + 1)
                sp.dma_start(out[0, q * P:(q + 1) * P, :], yb[:, q, :]).then_inc(sem("out_sent"), 16)
            sp.wait_ge(sem("out_sent"), 16 * NT)

        @block_.gpsimd
        def _(pool):
            nc.gpsimd.memset(cs, 0.0).then_inc(sem("cleared"), 1)
            nc.gpsimd.memset(eps, EPS).then_inc(sem("cleared"), 1)
            nc.gpsimd.memset(qscale, -0.5 * math.log(P)).then_inc(sem("cleared"), 1)
            pool.wait_ge(sem("tables_in"), 144)
            nc.gpsimd.partition_broadcast(lamb.rearrange("p a b -> p (a b)"), lamv[0:1].rearrange("p a b -> p (a b)"), P).then_inc(sem("broadcast"), 1)
            pool.wait_ge(sem("mixf_mm"), H)
            for m in range(2):
                o = HD * (1 - m)
                nc.gpsimd.memset(qz[o:o + HD, :, m, :], 0.0).then_inc(sem("cleared"), 1)
            for i in range(H * NT):
                pool.wait_ge(sem("pr_scales"), i + 1)
                e1 = ex[:, i % 2, 1, :]
                nc.gpsimd.tensor_scalar(e1, e1, rz[:, 1:2], None, ALU.mult).then_inc(sem("map1_scaled"), 1)
            pool.wait_ge(sem("mod_rows"), 2)
            pool.wait_ge(sem("rotary_q"), 2 * H + H)
            for n in range(2):
                nc.gpsimd.partition_broadcast(gt1b[:, n * 512:n * 512 + 512], modr[32 * n:32 * n + 1, 1, :], P).then_inc(sem("broadcast"), 1)
                pool.wait_ge(sem("broadcast"), n + 2)

            pool.wait_ge(sem("mod_rows"), 3)
            pool.wait_ge(sem("mixa"), H)
            pool.wait_ge(sem("rows_in"), 96)
            flat = rowt.rearrange("p a b -> p (a b)")
            for dst, src in ((gffb, flat[0:1, 0:D]), (gfb, flat[0:1, D:2 * D])):
                nc.gpsimd.partition_broadcast(dst, src, P).then_inc(sem("broadcast"), 1)
            pool.wait_ge(sem("broadcast"), 5)
            for i, (dst, r, j) in enumerate(((gsb, 2, 0), (sh2b, 1, 2), (gt2b, 2, 2))):
                for n in range(2):
                    p0 = 32 * (j + n)
                    nc.gpsimd.partition_broadcast(dst[:, n * 512:n * 512 + 512], modr[p0:p0 + 1, r, :], P).then_inc(sem("broadcast"), 1)
                    pool.wait_ge(sem("broadcast"), 2 * i + n + 6)
            nc.gpsimd.memset(fill, NO_TOKEN).then_inc(sem("cleared"), 1)
            pool.wait_ge(sem("rows_in"), 96)
            nc.gpsimd.partition_broadcast(rbias, rbias[0:1], P).then_inc(sem("broadcast"), 1)
            pool.wait_ge(sem("cleared"), CLEARED["fill"])
            table = scratch["table"]
            pool.dma_start(table.rearrange("(p n) o -> p (n o)", p=P), fill.bitcast(U32)).then_inc(sem("table_empty"), 16)
            pool.wait_ge(sem("table_empty"), 16)
            pool.wait_ge(sem("vector_step"), VECTOR_STEP["slots"] + 1)
            for n in range(2 * NT):
                pool.indirect_dma_start(out=table, out_offset=bass.IndirectOffsetOnAxis(ap=slot[:, n:n + 1].bitcast(U32), axis=0),
                                        in_=val[:, n:n + 1].bitcast(U32), in_offset=None,
                                        bounds_check=ROUNDS * CAP * NEXP - 1, oob_is_err=False).then_inc(sem("table_set"), 16)
            pool.wait_ge(sem("table_set"), 32 * NT)
            for n in range(2):
                pool.dma_start(tabs[64 * n:64 * n + 64, 0, :].bitcast(U32), table.rearrange("(p n) o -> p (n o)", p=CAP)).then_inc(sem("table_in"), 16)
            pool.wait_ge(sem("h2_out"), 16 * NT)
            nc.gpsimd.memset(xg, 0.0).then_inc(sem("cleared"), 1)
            nc.gpsimd.memset(ye, 0.0).then_inc(sem("cleared"), 1)
            nc.gpsimd.memset(ixw.bitcast(I32), NO_TOKEN).then_inc(sem("cleared"), 1)
            nc.gpsimd.memset(stage, 0.0).then_inc(sem("cleared"), 1)
            pool.wait_ge(sem("cleared"), CLEARED["xg"])
            pool.wait_ge(sem("vector_step"), VECTOR_STEP["row_numbers"] + 1)

            last_read = pool.to_reg(2 * S - 1)
            last_write = pool.to_reg(4 * S - 1)

            def pick(dst, w, k, u):
                nc.gpsimd.tensor_copy(dst[:, u, :], tabs[:, w, bass.ds(k, 1)].bitcast(U32)).then_inc(sem("rows_picked"), 1)

            def gather(u):
                pool.indirect_dma_start(out=xg[:, u, :], out_offset=None, in_=scratch["h2"],
                                        in_offset=bass.IndirectOffsetOnAxis(ap=ixr[:, u, :], axis=0),
                                        bounds_check=last_read, oob_is_err=False).then_inc(sem(f"xg_in_{u}"), 16)

            def scatter(u):
                pool.indirect_dma_start(out=scratch["y"], out_offset=bass.IndirectOffsetOnAxis(ap=ixw[:, u, :], axis=0),
                                        in_=ye[:, u, :], in_offset=None,
                                        bounds_check=last_write, oob_is_err=False).then_inc(sem(f"ye_out_{u}"), 16)

            for u in range(2):
                pick(ixr, 1, u, u)
                pool.wait_ge(sem("rows_picked"), u + 1)
                gather(u)
                scatter(u)
            with pool.Fori(0, NEXP // 2) as i:
                for u in range(2):
                    pool.wait_ge(sem("xg_turned"), 2 * i + (u + 1))
                    pool.wait_ge(sem(f"xg_in_{u}"), 16 * i + 16)
                    pool.wait_ge(sem("vector_step"), VECTOR_STEP["row_numbers"] + 1)
                    pick(ixr, 1, 2 * i + (u + 2), u)
                    pool.wait_ge(sem("rows_picked"), 4 * i + (2 * u + 3))
                    pool.sem_inc(sem("seen"), 1)
                    gather(u)
                    pool.wait_ge(sem(f"ye_out_{u}"), 16 * i + 16)
                    pool.wait_ge(sem("vector_step"), VECTOR_STEP["row_numbers"] + 1)
                    pick(ixw, 2, 2 * i + u, u)
                    pool.wait_ge(sem("rows_picked"), 4 * i + (2 * u + 4))
                    pool.wait_ge(sem("ye"), 2 * i + (u + 2))
                    pool.sem_inc(sem("seen"), 1)
                    scatter(u)
            for u in range(2):
                pool.wait_ge(sem(f"xg_in_{u}"), 16 * (NEXP // 2 + 1))
                pool.wait_ge(sem(f"ye_out_{u}"), 16 * (NEXP // 2 + 1))
            more = pool.value_load(flag[0:1, 0:1], min_val=0, max_val=1)
            with pool.If(more > 0):
                with pool.Fori(1, ROUNDS) as r:
                    with pool.Fori(0, NEXP) as e:
                        n = NEXP * r + e - NEXP
                        pick(ixr, 1, r * NEXP + e, 0)
                        pick(ixw, 2, r * NEXP + e, 0)
                        pool.wait_ge(sem("rows_picked"), 2 * n + (2 * NEXP + 4))
                        pool.sem_inc(sem("seen"), 1)
                        gather(0)
                        pool.wait_ge(sem("more_ye"), n + 2)
                        pool.sem_inc(sem("seen"), 1)
                        scatter(0)
                        pool.wait_ge(sem("ye_out_0"), 16 * n + 16 * (NEXP // 2 + 2))
                        pool.wait_ge(sem("vector_step"), VECTOR_STEP["row_numbers"] + 1)
            y = scratch["y"].rearrange("(q p k c) n -> q p (k c n)", p=P, k=2, c=2)
            for q in range(NT):
                pool.dma_start(ygo[:, q, :, :].rearrange("p k n -> p (k n)"), y[q]).then_inc(sem(f"y_in_{q // 2}"), 16)
            pool.wait_ge(sem("x2"), NT)
            nc.gpsimd.memset(wab, 0.0).then_inc(sem("cleared"), 1)
            pool.wait_ge(sem("x3"), NT)
            for m in range(2):
                o = HD * (1 - m)
                pool.wait_ge(sem("cleared"), CLEARED["qs"] - 2 + m)
                nc.gpsimd.memset(qs.rearrange("p (c m) n -> p c m n", m=2)[o:o + HD, :, m, :], 0.0).then_inc(sem("cleared"), 1)

            def later_queries(x, signal):
                nc.gpsimd.affine_select(out=x[:, 0:P], in_=x[:, 0:P], compare_op=ALU.is_gt, fill=0.0, base=0,
                                        pattern=[[1, P]], channel_multiplier=-1).then_inc(sem(signal), 1)

            pool.wait_ge(sem("cleared"), CLEARED["qs"])
            for what, h in STICK_PLAN:
                for n, kb in enumerate(reversed(range(NT))):
                    if what == "z":
                        pool.wait_ge(sem("stick_sp"), 4 * h + n + 1)
                        later_queries(spz[kb], "sp_masked")
                    elif what == "suffix":
                        pool.wait_ge(sem("stick_probs"), 4 * h + n + 1)
                        later_queries(azz[kb], "probs_masked")
            causal = CAUSAL.unsqueeze(1).to_broadcast([P, NT, P])
            for pair in range(H // 2):
                for p in range(2):
                    h = 2 * pair + p
                    pool.wait_ge(sem("dec_exp"), h + 1)
                    nc.gpsimd.tensor_tensor(dec[:, p, :, :], dec[:, p, :, :], causal, ALU.mult).then_inc(sem("dec"), 1)
                for lv in range(1, 6):
                    for p in range(2):
                        n = (5 * pair + lv - 1) * 2 + p
                        pool.wait_ge(sem("solve_dve"), SOLVE_DVE["mt", 2 * pair + p])
                        if lv > 1:
                            pool.wait_ge(sem("solve_mm"), SOLVE_MM["y", 2 * pair + p, lv - 1])
                        nc.gpsimd.tensor_tensor(Mo[:, p, :, :], MT[:, p, :, :], JOIN[lv].unsqueeze(1).to_broadcast([P, NT, P]), ALU.mult)\
                            .then_inc(sem("mo"), 1)
            pool.wait_ge(sem("solve_mm"), SOLVE_MM["w", H - 1])
            nc.gpsimd.memset(state, 0.0).then_inc(sem("cleared"), 1)
            nc.gpsimd.memset(vE, 0.0).then_inc(sem("cleared"), 1)
            nc.gpsimd.memset(vO, 0.0).then_inc(sem("cleared"), 1)
            pool.wait_ge(sem("prow_in"), 16)
            nc.gpsimd.partition_broadcast(postb, prow[0:1, :], P).then_inc(sem("broadcast"), 1)

        @block_.scalar
        def _(act):
            act.add_instruction(mybir.InstLoadActFuncSet(name=nc.get_next_instruction_name(), act_func_set_id=EXP_AND_LOG, ins=[], outs=[]))
            act.dma_start(c2[:, 0, :], a["c"][0].rearrange("(p k) -> p k", k=KD)).then_inc(sem("c_in"), 16)
            act.dma_start(c2[:, 1, :], a["c_ctx"].rearrange("(p k) -> p k", k=KD)).then_inc(sem("c_in"), 16)
            act.dma_start(xc[:, 0:NT, :], a["x"][0].rearrange("(q p) n -> p q n", p=P)).then_inc(sem("x_in"), 16)
            act.dma_start(xc[:, NT:NT + NC, :], a["ctx"][0].rearrange("(q p) n -> p q n", p=P)).then_inc(sem("ctx_in"), 16)
            act.dma_start(sq, t["squares"][:, 0:6, :]).then_inc(sem("tables_in"), 16)
            act.wait_ge(sem("vector_step"), VECTOR_STEP["modr_zero"] + 1)
            b_ada = a["b_ada"].rearrange("o (r j n) -> (o j) r n", j=4, n=512)
            for m in range(2):
                act.dma_start(modr[m:P:32, :, :], b_ada).then_inc(sem("tables_in"), 16)
            act.dma_start(modr[2:2 + 33:32, 0, :], a["g_mix_norm"].rearrange("o (j n) -> (o j) n", n=512)).then_inc(sem("tables_in"), 16)
            for n, name in enumerate(("lambda_q1", "lambda_k1", "lambda_q2", "lambda_k2")):
                act.dma_start(lamv[0:1, n, :], a[name]).then_inc(sem("tables_in"), 16)
            act.dma_start(wf.rearrange("p (g d) -> p g d", g=H), a["w_fourier"][0].rearrange("g c d -> c g d")).then_inc(sem("tables_in"), 16)
            act.dma_start(rope, t["rope"]).then_inc(sem("more_tables_in"), 16)
            act.dma_start(gsub, a["g_subln"].rearrange("o d -> d o")).then_inc(sem("more_tables_in"), 16)
            act.dma_start(dft_seq, t["dft_seq"]).then_inc(sem("more_tables_in"), 16)

            act.wait_ge(sem("c_in"), 32)
            nc.scalar.activation(ce, c2.rearrange("p m k -> p (m k)"), ACT.Exp, scale=-1.0).then_inc(sem("small_exp"), 1)
            for n in range(NT + NC):
                act.wait_ge(sem("x_in" if n < NT else "ctx_in"), 16)
                act_link(act, nc.scalar.activation(banks(6, D), xc[:, n, :], ACT.Square, accum_out=ss[:, n:n + 1]))
            act.wait_ge(sem("cleared"), CLEARED["qscale"])
            act_link(act, nc.scalar.activation(lnss, ss, ACT.Ln, scale=1.0 / D, bias=eps))
            nc.scalar.activation(rstd, lnss, ACT.Exp, scale=-0.5).then_inc(sem("rms"), 1)
            act.wait_ge(sem("vector_step"), VECTOR_STEP["lambda_sums"] + 2)
            nc.scalar.activation(lame, lams, ACT.Exp).then_inc(sem("small_exp"), 1)
            act.wait_ge(sem("vector_step"), VECTOR_STEP["gains"] + 2)
            for k in range(KD):
                act.wait_ge(sem("ctx_turned"), k + 1)
                nc.scalar.activation(hcT[:, k, :], bank(5 + k % 3, CTX), ACT.Identity,
                                     scale=gain[:, 1, k:k + 1], bias=mhc[:, k // 4, k % 4, 1:2]).then_inc(sem("hcT"), 1)
            for n in range(2 * NT):
                act.wait_ge(sem("fcs_mm"), n + 1)
                nc.scalar.copy(fcs[:, n // 2, 2 * (n % 2):2 * (n % 2) + 2, :].rearrange("p a b -> p (a b)"), bank(4 + n % 2)).then_inc(sem("fcs"), 1)
            for n in range(KT):
                if n < KT - 1:
                    act.wait_ge(sem("v_mm"), n + 1)
                else:
                    act.wait_ge(sem("blocks_used"), B_V + 1)
                nc.scalar.copy(v[:, n, :], bank(6 + n % 2)).then_inc(sem("v"), 1)
            for n in range(2 * H):
                if n == H - 1:
                    act.wait_ge(sem("blocks_used"), B_Q + 1)
                else:
                    act.wait_ge(sem("qk_mm"), n + 1 if n < H else n)
                if n >= 2:
                    act.wait_ge(sem("rotary_mm"), n - 1)
                    act.wait_ge(sem("qcos"), n - 1)
                nc.scalar.activation(qraw[:, n % 2, :], bank(n % 2), ACT.Copy, scale=0.125 if n < H else 1.0).then_inc(sem("qraw"), 1)
                if n >= H:
                    if n < 2 * H - 1:
                        act.wait_ge(sem("kc_mm"), n - H + 1)
                    else:
                        act.wait_ge(sem("blocks_used"), B_K + 1)
                    nc.scalar.copy(kT[:, n - H, 0:CTX], bank(4 + n % 2, CTX)).then_inc(sem("kc"), 1)
            act.wait_ge(sem("mixf_mm"), H)
            act.dma_start(x1, a["x"][0].rearrange("(q p) n -> p q n", p=P)).then_inc(sem("x_again"), 16)
            for h in range(H):
                for q in range(NT):
                    i = h * NT + q
                    for m in range(2):
                        act.wait_ge(sem("score_max"), 2 * i + m + 1)
                        if i >= 2:
                            act.wait_ge(sem("pr_turned"), i - 1)
                        nc.scalar.activation(ex[:, i % 2, m, :], banks(2 * m, NKEY), ACT.Exp, bias=nmax[:, m:m + 1],
                                             accum_out=zsum[:, 2 * (i % 2) + m:2 * (i % 2) + m + 1]).then_inc(sem("exps"), 1)
                    if q == 2 and h >= 1:
                        act_subln(act, h - 1)
                    if i >= 1:
                        act_prT(act, i - 1)
            act_prT(act, H * NT - 1)
            act_subln(act, H - 1)
            act.wait_ge(sem("mixa"), H)
            act.dma_start(rowt[0:1, 0, :], a["g_ffn_norm"]).then_inc(sem("rows_in"), 16)
            act.dma_start(rowt[0:1, 1, :], a["g_final"].rearrange("(o n) -> o n", o=1)).then_inc(sem("rows_in"), 16)
            act.dma_start(wr[:, :, 0:NGRP], a["w_router_group"][0].rearrange("(k p) n -> p k n", p=P)).then_inc(sem("rows_in"), 16)
            act.dma_start(wr[:, :, NGRP:36], a["w_router_expert"][0].rearrange("(k p) n -> p k n", p=P)).then_inc(sem("rows_in"), 16)
            act.dma_start(rbias[0:1, 0:NGRP], a["b_router_group"]).then_inc(sem("rows_in"), 16)
            act.dma_start(rbias[0:1, NGRP:36], a["b_router_expert"]).then_inc(sem("rows_in"), 16)
            for q in range(NT):
                act.wait_ge(sem("x1_half"), NT + q + 1)
                act_link(act, nc.scalar.activation(banks(4, D), x1[:, q, :], ACT.Square, accum_out=ss[:, q:q + 1]))
                act_link(act, nc.scalar.activation(lnss[:, q:q + 1], ss[:, q:q + 1], ACT.Ln, scale=1.0 / D, bias=eps))
                nc.scalar.activation(rstd[:, q:q + 1], lnss[:, q:q + 1], ACT.Exp, scale=-0.5).then_inc(sem("rms"), 1)
            act.wait_ge(sem("broadcast"), BROADCAST["ffn"])
            act.dma_start(rcon, t["router"]).then_inc(sem("rcon_in"), 16)
            for q in range(NT):
                act.wait_ge(sem("h2"), q + 1)
                act.dma_start(scratch["h2"].rearrange("(q p c) n -> q p (c n)", q=NT, c=2)[q], h2[:, q, :]).then_inc(sem("h2_out"), 16)
                for z in range(2):
                    act.wait_ge(sem("h2_turned"), 2 * q + z + 1)
                    nc.scalar.copy(h2T[:, 4 * z:4 * z + 4, q * P:(q + 1) * P], bank(4 + z).rearrange("p (k n) -> p k n", k=4)).then_inc(sem("h2T"), 1)
                act.wait_ge(sem("logits_mm"), q + 1)
                nc.scalar.copy(lgT[0:36, q * P:(q + 1) * P], ps[0:36, 6, q * P:(q + 1) * P]).then_inc(sem("logitsT"), 1)
            act.wait_ge(sem("router_diff"), 1)
            nc.scalar.activation(dg, dg, ACT.Exp).then_inc(sem("small_exp"), 1)
            act.wait_ge(sem("router_diff"), 2)
            nc.scalar.activation(d2, d2, ACT.Exp).then_inc(sem("small_exp"), 1)

            act.wait_ge(sem("cleared"), CLEARED["stage"])
            act.wait_ge(sem("tensor_step"), TENSOR_STEP["ranks_mm"] + 1)
            act.dma_start(sq2, t["squares"][:, 6:15, :]).then_inc(sem("sq2_in"), 16)
            act.dma_start(stage[0:48, :], a["conv_w_2"][0].rearrange("i (c p) -> (i c) p", p=P)).then_inc(sem("columns_in"), 16)
            act.dma_start(stage[48:56, :], a["pre_norm_w_2"].rearrange("o (k p) -> (o k) p", p=P)).then_inc(sem("columns_in"), 16)
            act.dma_start(dtb[0:4], a["dt_bias_2"].rearrange("o h -> h o")).then_inc(sem("columns_in"), 16)
            act.dma_start(alog[0:4], a["a_log_2"].rearrange("o h -> h o")).then_inc(sem("columns_in"), 16)
            act.dma_start(gnw, a["gdn_norm_w_2"].rearrange("o d -> d o")).then_inc(sem("columns_in"), 16)

            for name in ("ye", "more_ye", "more_done"):
                act.sem_inc(sem(name), 1)
            with act.Fori(0, NEXP // 2) as i:
                for u in range(2):
                    act.wait_ge(sem("blocks_used"), 6 * i + (B_MOE + 3 * u + 1))
                    nc.scalar.activation(ge[:, 0, :], bank(2, 256), ACT.Exp, scale=-1.0).then_inc(sem("gate_exp"), 1)
            more = act.value_load(flag[0:1, 0:1], min_val=0, max_val=1)
            with act.If(more > 0):
                with act.Fori(0, (ROUNDS - 1) * NEXP) as n:
                    act.wait_ge(sem("more_gate"), n + 1)
                    nc.scalar.activation(ge[:, 0, :], bank(2, 256), ACT.Exp, scale=-1.0).then_inc(sem("gate_exp"), 1)
            for kind, q in NORMS:
                ready, sums, logs, out_ = ("x2", ss, lnss, rstd) if kind == "final" else ("x3", ss3, ln3, rs3)
                act.wait_ge(sem(ready), q + 1)
                act_link(act, nc.scalar.activation(banks(4, D), x1[:, q, :], ACT.Square, accum_out=sums[:, q:q + 1]))
                act_link(act, nc.scalar.activation(logs[:, q:q + 1], sums[:, q:q + 1], ACT.Ln, scale=1.0 / D, bias=eps))
                nc.scalar.activation(out_[:, q:q + 1], logs[:, q:q + 1], ACT.Exp, scale=-0.5).then_inc(sem("rms"), 1)

            act.wait_ge(sem("cleared"), CLEARED["wab"])
            for n in range(2):
                c0 = COLS2["ab"] + H * n
                act.dma_start(wab[:, :, 32 * n:32 * n + H], a["w_in_2"][0, :, c0:c0 + H].rearrange("(k p) n -> p k n", p=P)).then_inc(sem("wab_in"), 16)
            def second_wait(n, mm, first):
                if n % 4 == 3:
                    act.wait_ge(sem("blocks_used"), B_SECOND + first + n // 4 + 1)
                else:
                    act.wait_ge(sem(mm), n + 1 - (n + 1) // 4)

            for k in range(KD):
                act.wait_ge(sem("h3_turned"), k + 1)
                act.wait_ge(sem("vector_step"), VECTOR_STEP["prew"] + 1)
                nc.scalar.activation(h3T[:, k, :], bank(k % 4), ACT.Copy, scale=prew[:, k:k + 1]).then_inc(sem("h3T"), 1)
            def rows_ab(act):
                act.wait_ge(sem("columns_in"), 80)
                nc.scalar.activation(nea[0:4], alog[0:4], ACT.Exp).then_inc(sem("small_exp"), 1)
                act.wait_ge(sem("vector_step"), VECTOR_STEP["dt_abs"] + 1)
                act_link(act, nc.scalar.activation(trow2[0:4], trow2[0:4], ACT.Exp, scale=-1.0))
                nc.scalar.activation(trow2[0:4], trow2[0:4], ACT.Ln, bias=ONES[0:4, 0:1]).then_inc(sem("small_exp"), 1)
                act.wait_ge(sem("vector_step"), VECTOR_STEP["rows_zero"] + 1)
                nc.scalar.activation(trow[32:36], ps[32:36, 0, :], ACT.Exp, scale=-1.0).then_inc(sem("small_exp"), 1)
                act.wait_ge(sem("vector_step"), VECTOR_STEP["to_last"] + 1)
                nc.scalar.activation(rows[64:68], trow[0:4], ACT.Exp).then_inc(sem("rows"), 1)

            act.wait_ge(sem("cleared"), CLEARED["qs"])
            for n in range(12):
                if n == 8:
                    rows_ab(act)
                second_wait(n, "qkv_mm", 0)
                b = 5 + n % 3
                if n < 4:
                    nc.scalar.activation(qs[0:HD, 2 * n, :], ps[0:HD, b, :], ACT.Copy, scale=0.125)
                    ins = nc.scalar.activation(qs[HD:P, 2 * n + 1, :], ps[HD:P, b, :], ACT.Copy, scale=0.125)
                else:
                    ins = nc.scalar.copy((ks, vs)[n // 4 - 1][:, n % 4, :], bank(b))
                ins.then_inc(sem("qkv_out"), 1)

            def act_z(h):
                for n, kb in enumerate(reversed(range(NT))):
                    act.wait_ge(sem("stick_mm"), 4 * h + n + 1)
                    act_link(act, nc.scalar.activation(ezz[kb], bank(kb, S - kb * P), ACT.Abs))
                    act_link(act, nc.scalar.activation(ezz[kb], ezz[kb], ACT.Exp, scale=-1.0))
                    nc.scalar.activation(ezz[kb], ezz[kb], ACT.Ln, bias=ONES[:, 0:1]).then_inc(sem("stick_ln"), 1)

            def act_suffix(h):
                if h:
                    act.wait_ge(sem("stick_o"), h)
                for n, kb in enumerate(reversed(range(NT))):
                    act.wait_ge(sem("stick_sum"), 4 * h + n + 1)
                    nc.scalar.activation(azz[kb], bank(kb, S - kb * P), ACT.Exp).then_inc(sem("stick_probs"), 1)

            def act_fill(f):
                if f < 4 or f >= 16:
                    second_wait(f, "fill_mm", 3)
                    src = bank(5 + f % 3)
                else:
                    act.wait_ge(sem("convolved"), f - 3)
                    src = gdn[f // 4 - 1][:, f % 4, :]
                if f >= 2:
                    act.wait_ge(sem("silu_done"), f - 1)
                nc.scalar.activation(cv[:, f % 2, :], src, ACT.Exp, scale=-1.0).then_inc(sem("silu_exp"), 1)

            for what, n in STICK_PLAN:
                if what == "z":
                    act_z(n)
                elif what == "suffix":
                    act_suffix(n)
                elif what == "fill":
                    act_fill(n)
            def act_merge(f):
                if f % 4 < 3:
                    act.wait_ge(sem("merge_mm"), f + 1 - (f + 1) // 4)
                else:
                    act.wait_ge(sem("blocks_used"), B_SECOND + (9, 11)[f // 4])
                act_link(act, nc.scalar.activation(merged[:, f, :], bank(4 + 2 * (f % 2)), ACT.Exp, scale=-1.0))
                act_link(act, nc.scalar.activation(merged[:, f, :], merged[:, f, :], ACT.Ln, bias=ONES[:, 0:1]))
                nc.scalar.activation(merged[:, f, :], merged[:, f, :], ACT.Exp, scale=-1.0).then_inc(sem("merge_exp"), 1)

            def merge_at(*point):
                if point in MERGE_AT and MERGE_AT[point] % 3 == 2:
                    act_merge(MERGE_AT[point] // 3)

            act.wait_ge(sem("colsab"), 1)
            nc.scalar.activation(egc, colsab[:, :, 0, :], ACT.Exp).then_inc(sem("small_exp"), 1)
            for n in range(2 * H):
                src = (gk, gq)[n // H][:, n % H, :]
                act.wait_ge(sem("silu_done"), 16)
                if n >= 2:
                    act.wait_ge(sem("gss_mm"), n - 1)
                nc.scalar.activation(cu[:, n % 2, :], src, ACT.Square).then_inc(sem("gsq"), 1)
                if n >= 1:
                    act_norm(act, n - 1)
                merge_at("norm", n)
            act_norm(act, 2 * H - 1)
            for pair in range(H // 2):
                for p in range(2):
                    h = 2 * pair + p
                    act.wait_ge(sem("solve_mm"), SOLVE_MM["grow", h])
                    if pair:
                        act.wait_ge(sem("solve_dve"), SOLVE_DVE["qe", h - 2])
                    nc.scalar.activation(egrow[:, p, :], bank(2 * p), ACT.Exp).then_inc(sem("egrow"), 1)
                    act.wait_ge(sem("solve_dve"), SOLVE_DVE["dec", h])
                    d_ = dec[:, p, :, :].rearrange("p a b -> p (a b)")
                    nc.scalar.activation(d_, d_, ACT.Exp).then_inc(sem("dec_exp"), 1)
                for n in range(4):
                    merge_at("solve", pair, n)
                for lv in range(1, 6):
                    for p in range(2):
                        n = (5 * pair + lv - 1) * 2 + p
                        act.wait_ge(sem("solve_mm"), SOLVE_MM["y", 2 * pair + p, lv])
                        if lv > 1:
                            act.wait_ge(sem("solve_mm"), SOLVE_MM["u", 2 * pair + p, lv - 1])
                        nc.scalar.copy(Yl[:, p, :, :].rearrange("p a b -> p (a b)"), bank(2 * p + 1)).then_inc(sem("yl"), 1)
                for p in range(2):
                    h = 2 * pair + p
                    act.wait_ge(sem("solve_mm"), SOLVE_MM["u", h])
                    nc.scalar.copy(gv[:, h, :], bank(2 * p)).then_inc(sem("u"), 1)
            for c in range(S // CHUNK):
                o = slice(CHUNK * (c % 2), CHUNK * (c % 2) + CHUNK)
                merge_at("chunk", c)
                act.wait_ge(sem("chunk_mm"), 3 * c + 3)
                nc.scalar.copy(og[o, c // 2, :], ps[o, 2 + c % 2, :]).then_inc(sem("og"), 1)
            act_merge(KD - 2)
            act_merge(KD - 1)
            act.wait_ge(sem("oss2"), NT)
            act_link(act, nc.scalar.activation(oln2, oss2, ACT.Ln, scale=1.0 / P, bias=eps))
            nc.scalar.activation(ors2, oln2, ACT.Exp, scale=-0.5).then_inc(sem("rms"), 1)
            act.wait_ge(sem("og_turned"), H)
            act.dma_start(prow[0:1, :], a["post_norm_w_2"]).then_inc(sem("prow_in"), 16)
            for n in range(KD, 2 * KD):
                f = n % KD
                if f % 4 < 3:
                    act.wait_ge(sem("merge_mm"), n + 1 - (n + 1) // 4)
                else:
                    act.wait_ge(sem("blocks_used"), B_SECOND + (9, 11, 12, 14)[n // 4])
                if n >= 2:
                    act.wait_ge(sem("merge_out"), n - 1)
                nc.scalar.activation(sig[:, n % 2, 0, :], bank(2 * (f % 4)), ACT.Exp, scale=-1.0).then_inc(sem("merge_exp"), 1)
            act.wait_ge(sem("merged"), KD)
            for q in range(NT):
                act.wait_ge(sem("y2_mm"), q + 1)
                act_link(act, nc.scalar.activation(junk, banks(4 * (q % 2), D), ACT.Square, accum_out=fss[:, q:q + 1]))
                act_link(act, nc.scalar.activation(fln[:, q:q + 1], fss[:, q:q + 1], ACT.Ln, scale=1.0 / D, bias=eps))
                nc.scalar.activation(frs[:, q:q + 1], fln[:, q:q + 1], ACT.Exp, scale=-0.5).then_inc(sem("rms"), 1)


        @block_.tensor
        def _(pe):
            def arrived(n):
                pe.wait_ge(sem(f"block_in_{n % RING}"), 16 * (n // RING + 1))

            def used(ins):
                return ins.then_inc(sem("blocks_used"), 1)

            def ada_round(r, blk, b):
                for j in range(4):
                    arrived(blk + j)
                for k in range(KD):
                    for j in range(4):
                        mm = pe.matmul(ps[32 * j:32 * j + 32, b, :], cs[:, k, :], block(blk + j)[:, k, :],
                                       start=k == 0, stop=k == KD - 1)
                        if k == KD - 1:
                            used(mm)

            pe.wait_ge(sem("vector_step"), VECTOR_STEP["silu_c"] + 1)
            ada_round(0, B_ADA0, 0)
            pe.wait_ge(sem("mod_rows"), 1)
            pe.wait_ge(sem("tables_in"), 144)
            for q in range(4):
                mm = pe.transpose(ps[:, 1, q * P:(q + 1) * P], modr[:, 0, q * P:(q + 1) * P], IDENT)
            mm.then_inc(sem("tensor_step"), 1)
            pe.wait_ge(sem("tables_in"), 144)
            pe.matmul(bank(2), COS, wf, start=True, stop=True)
            pe.matmul(bank(3), SIN, wf, start=True, stop=True).then_inc(sem("tensor_step"), 1)
            pe.wait_ge(sem("vector_step"), VECTOR_STEP["normed"] + NT + NC)
            pe.wait_ge(sem("vector_step"), VECTOR_STEP["wcs"] + 2)
            for k in range(KD):
                if k >= 3:
                    pe.wait_ge(sem("hT"), k - 2)
                for n in range(NT):
                    mm = pe.transpose(ps[:, 2 + k % 3, n * P:(n + 1) * P], xc[:, n, k * P:(k + 1) * P], IDENT)
                mm.then_inc(sem("x_turned"), 1)
                if k >= 3:
                    pe.wait_ge(sem("hcT"), k - 2)
                for n in range(NC):
                    mm = pe.transpose(ps[:, 5 + k % 3, n * P:(n + 1) * P], xc[:, NT + n, k * P:(k + 1) * P], IDENT)
                mm.then_inc(sem("ctx_turned"), 1)
            arrived(B_F)
            pe.wait_ge(sem("hT"), KD)
            for g in range(H):
                if g >= 2:
                    pe.wait_ge(sem("fT"), g - 1)
                for k in range(KD):
                    mm = pe.matmul(bank(g % 2), block(B_F)[:, k, g * P:(g + 1) * P], hT[:, k, :], start=k == 0, stop=k == KD - 1)
                mm.then_inc(sem("f_mm" if g < H - 1 else "blocks_used"), 1)
            pe.wait_ge(sem("fT"), H)
            pe.wait_ge(sem("hcT"), KD)
            for n in range(2 * NT):
                if n >= 2:
                    pe.wait_ge(sem("fcs"), n - 1)
                for g in range(2):
                    gg = 2 * (n % 2) + g
                    mm = pe.matmul(ps[:, 4 + n % 2, g * 256:(g + 1) * 256], fT[:, gg, n // 2 * P:(n // 2 + 1) * P],
                                   wcs[:, gg, :, :].rearrange("p a b -> p (a b)"), start=True, stop=True)
                mm.then_inc(sem("fcs_mm"), 1)
            arrived(B_V)
            for n in range(KT):
                if n >= 2:
                    pe.wait_ge(sem("v"), n - 1)
                src, o = (hcT, n) if n < NC else (hT, n - NC)
                for k in range(KD):
                    mm = pe.matmul(bank(6 + n % 2), src[:, k, o * P:(o + 1) * P], block(B_V)[:, k, :], start=k == 0, stop=k == KD - 1)
                mm.then_inc(sem("v_mm" if n < KT - 1 else "blocks_used"), 1)
            pe.wait_ge(sem("more_tables_in"), 48)
            pe.wait_ge(sem("fcs"), 2 * NT)
            for g in range(H):
                if g >= 2:
                    pe.wait_ge(sem("mixf"), g - 1)
                for z in range(2):
                    for n in range(NT):
                        mm = pe.matmul(bank(2 + g % 2), fcs[:, n, g, z * P:(z + 1) * P], dft_seq[:, z, n, :],
                                       start=z + n == 0, stop=z == 1 and n == NT - 1)
                mm.then_inc(sem("mixf_mm"), 1)
            pe.wait_ge(sem("more_tables_in"), 48)

            def rotate(n):
                pe.wait_ge(sem("qraw"), n + 1)
                pe.wait_ge(sem("mixf"), H)
                if n >= 2:
                    pe.wait_ge(sem("rotary_q"), {True: 2 * (n - 1), False: 2 * H + n - 1 - H}[n - 1 <= H])
                pe.matmul(bank(2 + n % 2), ROT, qraw[:, n % 2, :], start=True, stop=True).then_inc(sem("rotary_mm"), 1)

            for n in range(2 * H):
                blk = B_Q if n < H else B_K
                c = n % H
                arrived(blk)
                if n >= 2:
                    pe.wait_ge(sem("qraw"), n - 1)
                for k in range(KD):
                    mm = pe.matmul(bank(n % 2), block(blk)[:, k, c * P:(c + 1) * P], hT[:, k, :], start=k == 0, stop=k == KD - 1)
                mm.then_inc(sem("qk_mm" if n != H - 1 else "blocks_used"), 1)
                if n >= H:
                    if n >= H + 2:
                        pe.wait_ge(sem("kc"), n - H - 1)
                    for k in range(KD):
                        mm = pe.matmul(bank(4 + n % 2, CTX), block(blk)[:, k, c * P:(c + 1) * P], hcT[:, k, :], start=k == 0, stop=k == KD - 1)
                    mm.then_inc(sem("kc_mm" if n < 2 * H - 1 else "blocks_used"), 1)
                if n >= 1:
                    rotate(n - 1)
            rotate(2 * H - 1)
            pe.wait_ge(sem("v"), KT)
            ada_round(1, B_ADA1, 6)
            ada_round(2, B_ADA1 + 4, 7)
            pe.wait_ge(sem("rotary_q"), 3 * H)
            pe.wait_ge(sem("cleared"), CLEARED["qz"])
            pe.wait_ge(sem("kc"), H)

            def scores(i):
                h, q = divmod(i, NT)
                for m in range(2):
                    if i >= 1:
                        pe.wait_ge(sem("exps"), 2 * (i - 1) + m + 1)
                    lq = qz[:, h, m, q * P:(q + 1) * P]
                    pe.matmul(bank(2 * m), lq, kT[:, h, 0:512], start=True, stop=True)
                    pe.matmul(bank(2 * m + 1, NKEY - 512), lq, kT[:, h, 512:NKEY], start=True, stop=True).then_inc(sem("scores"), 1)

            def weigh(i):
                h, q = divmod(i, NT)
                pe.wait_ge(sem("weights"), i + 1)
                for k in range(KT):
                    mm = pe.transpose(banks(4, NKEY)[:, k * P:(k + 1) * P], ex[:, i % 2, 0, k * P:(k + 1) * P], IDENT)
                mm.then_inc(sem("pr_turned"), 1)

            def attend(i):
                h, q = divmod(i, NT)
                pe.wait_ge(sem("prT"), i + 1)
                if q == 0 and h >= 1:
                    pe.wait_ge(sem("o_normed"), NT * h)
                for k in range(KT):
                    mm = pe.matmul(ps[:, 6, q * P:(q + 1) * P], prT[:, k, :], v[:, k, h * P:(h + 1) * P],
                                   start=k == 0, stop=k == KT - 1)
                mm.then_inc(sem("o_mm"), 1)

            def turn_o(h):
                if h >= 1:
                    pe.wait_ge(sem("mixa"), h)
                for q in range(NT):
                    pe.wait_ge(sem("o_normed"), NT * h + q + 1)
                    mm = pe.transpose(ps[:, 7, q * P:(q + 1) * P], oz(q), IDENT)
                mm.then_inc(sem("o_turned"), 1)

            pe.wait_ge(sem("mod_rows"), 3)
            scores(0)
            scores(1)
            for i in range(H * NT):
                if i + 2 < H * NT:
                    scores(i + 2)
                if i >= 1:
                    attend(i - 1)
                weigh(i)
                if i % NT == 2 and i > NT:
                    turn_o(i // NT - 1)
            attend(H * NT - 1)
            turn_o(H - 1)
            for n in range(2):
                arrived(B_WOUT + n)
                pe.wait_ge(sem("mixa"), H)
                for q in range(NT):
                    if n:
                        pe.wait_ge(sem("x1_half"), q + 1)
                    for k in range(KD):
                        src = mix_att if k < H else mix_fou
                        mm = pe.matmul(bank(q), src[:, k % H, q * P:(q + 1) * P], block(B_WOUT + n)[:, k, :], start=k == 0, stop=k == KD - 1)
                    mm.then_inc(sem("y1_mm" if q < NT - 1 else "blocks_used"), 1)
            pe.wait_ge(sem("rows_in"), 96)
            for q in range(NT):
                pe.wait_ge(sem("h2"), q + 1)
                for z in range(2):
                    if q == 0:
                        pe.wait_ge(sem("rms"), RMS["rstd1"] + NT)
                    else:
                        pe.wait_ge(sem("h2T"), 2 * q + z - 1)
                    for k in range(4):
                        mm = pe.transpose(ps[:, 4 + z, k * P:(k + 1) * P], h2[:, q, (4 * z + k) * P:(4 * z + k + 1) * P], IDENT)
                    mm.then_inc(sem("h2_turned"), 1)
                pe.wait_ge(sem("h2T"), 2 * q + 2)
                for k in range(KD):
                    mm = pe.matmul(ps[0:36, 6, q * P:(q + 1) * P], wr[:, k, :], h2T[:, k, q * P:(q + 1) * P], start=k == 0, stop=k == KD - 1)
                mm.then_inc(sem("logits_mm"), 1)
                pe.wait_ge(sem("logitsT"), q + 1)
                mm = pe.transpose(ps[:, 7, q * 36:q * 36 + 36], lgT[0:36, q * P:(q + 1) * P], IDENT[0:36, 0:36])
            mm.then_inc(sem("tensor_step"), 1)
            pe.wait_ge(sem("vector_step"), VECTOR_STEP["chosen"] + 1)
            pe.matmul(bank(0, P), BEFORE, As.rearrange("p a b -> p (a b)"), start=True, stop=False)
            pe.matmul(bank(0, P), ONES, pre[:, 0:NT, :].rearrange("p a b -> p (a b)"), start=False, stop=True)
            pe.matmul(bank(1, NEXP), ONES, pre[:, NT, :], start=True, stop=True).then_inc(sem("tensor_step"), 1)

            def turn_rows(u):
                for k in range(4):
                    mm = pe.transpose(ps[:, u, k * P:(k + 1) * P], xg[:, u, k * P:(k + 1) * P], IDENT)
                mm.then_inc(sem("xg_turned"), 1)

            def gate_up(u, wg, wu, signal_g, signal_u):
                for w, b, sg in ((wg, 2, signal_g), (wu, 3, signal_u)):
                    for k in range(KD):
                        for c in range(2):
                            mm = pe.matmul(ps[64 * c:64 * c + 64, b, 0:256], xeT[:, u, k % 4, 64 * (k // 4):64 * (k // 4) + 64],
                                           w[:, k, 256 * c:256 * c + 256], start=k == 0, stop=k == KD - 1)
                    mm.then_inc(sem(sg), 1)

            def turn_hidden(u):
                for b in range(2):
                    mm = pe.transpose(ps[:, 4, b * P:(b + 1) * P], he[:, u, b * P:(b + 1) * P], IDENT)
                mm.then_inc(sem("hidden_turned"), 1)

            def down(wd, signal):
                for k in range(4):
                    for c in range(2):
                        mm = pe.matmul(ps[64 * c:64 * c + 64, 6, :], heT[:, k % 2, 64 * (k // 2):64 * (k // 2) + 64],
                                       wd[:, k, 512 * c:512 * c + 512], start=k == 0, stop=k == 3)
                mm.then_inc(sem(signal), 1)

            pe.wait_ge(sem("vector_step"), VECTOR_STEP["slots"] + 1)
            pe.wait_ge(sem("xg_in_0"), 16)
            turn_rows(0)
            with pe.Fori(0, NEXP // 2) as i:
                for u in range(2):
                    for w in range(2):
                        pe.wait_ge(sem(f"block_in_{3 * u + w}"), 16 * i + 16 * (B_MOE // RING + 1))
                    pe.wait_ge(sem("xeT"), 2 * i + (u + 1))
                    gate_up(u, ring[:, 3 * u, :].rearrange("p (k n) -> p k n", k=KD),
                            ring[:, 3 * u + 1, :].rearrange("p (k n) -> p k n", k=KD), "blocks_used", "blocks_used")
                    pe.wait_ge(sem(f"xg_in_{1 - u}"), 16 * i + 16 * (u + 1))
                    turn_rows(1 - u)
                    pe.wait_ge(sem("hidden"), 2 * i + (u + 1))
                    turn_hidden(u)
                    pe.wait_ge(sem(f"block_in_{3 * u + 2}"), 16 * i + 16 * (B_MOE // RING + 1))
                    pe.wait_ge(sem("heT"), 2 * i + (u + 1))
                    pe.wait_ge(sem("ye"), 2 * i + (u + 1))
                    down(ring[:, 3 * u + 2, :].rearrange("p (k n) -> p k n", k=4), "blocks_used")
            more = pe.value_load(flag[0:1, 0:1], min_val=0, max_val=1)
            with pe.If(more > 0):
                with pe.Fori(0, (ROUNDS - 1) * NEXP) as n:
                    pe.wait_ge(sem("xg_in_0"), 16 * n + 16 * (NEXP // 2 + 2))
                    turn_rows(0)
                    pe.wait_ge(sem("more_in"), 48 * n + 48)
                    pe.wait_ge(sem("xeT"), n + (NEXP + 2))
                    gate_up(0, ring[:, 0, :].rearrange("p (k n) -> p k n", k=KD),
                            ring[:, 1, :].rearrange("p (k n) -> p k n", k=KD), "more_gate", "more_up")
                    pe.wait_ge(sem("hidden"), n + (NEXP + 1))
                    turn_hidden(0)
                    pe.wait_ge(sem("heT"), n + (NEXP + 1))
                    pe.wait_ge(sem("more_ye"), n + 1)
                    down(ring[:, 2, :].rearrange("p (k n) -> p k n", k=4), "more_done")
            def here(m):
                pe.wait_ge(sem(f"block_in_{m % RING2}"), 16 * (B_SECOND // RING + m // RING2 + 1))

            def place2(m):
                return ring[:, m % RING2, :].rearrange("p (k n) -> p k n", k=KD)

            pe.wait_ge(sem("columns_in"), 80)
            pe.wait_ge(sem("cleared"), CLEARED["stage"])
            pe.transpose(ps[:, 7, 0:P], stage, IDENT).then_inc(sem("tensor_step"), 1)
            for q in range(NT):
                pe.wait_ge(sem("h3"), q + 1)
            for k in range(KD):
                if k >= 4:
                    pe.wait_ge(sem("h3T"), k - 3)
                for q in range(NT):
                    mm = pe.transpose(ps[:, k % 4, q * P:(q + 1) * P], h3[:, q, k * P:(k + 1) * P], IDENT)
                mm.then_inc(sem("h3_turned"), 1)

            def by_feature(w, c, b):
                for k in range(KD):
                    mm = pe.matmul(bank(b), w[:, k, c * P:(c + 1) * P], h3T[:, k, :], start=k == 0, stop=k == KD - 1)
                return mm

            def by_token(w, q, b):
                for k in range(KD):
                    mm = pe.matmul(bank(b), h3T[:, k, q * P:(q + 1) * P], w[:, k, :], start=k == 0, stop=k == KD - 1)
                return mm

            pe.wait_ge(sem("h3T"), KD)
            for n in range(12):
                if n == 8:
                    pe.wait_ge(sem("wab_in"), 32)
                    pe.wait_ge(sem("cleared"), CLEARED["wab"])
                    for k in range(KD):
                        mm = pe.matmul(ps[0:64, 0, :], wab[:, k, :], h3T[:, k, :], start=k == 0, stop=k == KD - 1)
                    mm.then_inc(sem("tensor_step"), 1)
                if n % 4 == 0:
                    here(n // 4)
                if n >= 3:
                    pe.wait_ge(sem("qkv_out"), n - 2)
                mm = (by_feature if n < 8 else by_token)(place2(n // 4), n % 4, 5 + n % 3)
                mm.then_inc(sem("qkv_mm" if n % 4 < 3 else "blocks_used"), 1)

            def fill(f):
                if f % 4 == 0:
                    here(3 + f // 4)
                if f < 3:
                    pe.wait_ge(sem("qkv_out"), f + 10)
                else:
                    pe.wait_ge(sem("fill_out"), f - 2)
                mm = (by_feature if f < 16 else by_token)(place2(3 + f // 4), f % 4, 5 + f % 3)
                mm.then_inc(sem("fill_mm" if f % 4 < 3 else "blocks_used"), 1)

            def stick_scores(h):
                c = h // 2
                if h:
                    pe.wait_ge(sem("stick_probs"), 4 * h)
                for kb in reversed(range(NT)):
                    pe.matmul(bank(kb, S - kb * P), ks[:, c, kb * P:(kb + 1) * P], qs[:, h, kb * P:S], start=True, stop=True)\
                        .then_inc(sem("stick_mm"), 1)

            def stick_suffix(h):
                for kb in reversed(range(NT)):
                    pe.wait_ge(sem("sp_masked"), 4 * h + NT - kb)
                    for k2 in reversed(range(kb, NT)):
                        mm = pe.matmul(ps[:, kb, (k2 - kb) * P:S - kb * P], NEG_FROM if k2 == kb else NEG_ONES, spz[k2],
                                       start=False, stop=True, skip_group_check=True)
                    mm.then_inc(sem("stick_sum"), 1)

            def stick_attend(h):
                o = HD * (h % 2)
                if h >= 2 and h % 2 == 0:
                    pe.wait_ge(sem("osb"), h // 2)
                pe.wait_ge(sem("probs_masked"), 4 * h + NT)
                for kb in range(NT):
                    mm = pe.matmul(ps[o:o + HD, 4, kb * P:S], vs[:, kb, h * HD:(h + 1) * HD], azz[kb],
                                   start=kb == 0, stop=kb == NT - 1, skip_group_check=True)
                mm.then_inc(sem("stick_o"), 1)

            pe.wait_ge(sem("qkv_out"), 12)
            pe.wait_ge(sem("rows"), 3)
            pe.wait_ge(sem("cleared"), CLEARED["qs"])
            pe.wait_ge(sem("sq2_in"), 16)
            for what, n in STICK_PLAN:
                (stick_scores if what == "z" else stick_suffix if what == "suffix" else stick_attend if what == "attend" else fill)(n)

            pe.wait_ge(sem("stick_probs"), 4 * HS)
            for q in range(NT):
                mm = pe.transpose(ps[:, 1, q * P:(q + 1) * P], rows[:, q * P:(q + 1) * P], IDENT)
            mm.then_inc(sem("tensor_step"), 1)

            def merge_piece(n):
                f, part = divmod(n, 3)
                b = 4 + 2 * (f % 2)
                first = 8 + 2 * (f // 4)
                if part == 0:
                    if f >= 2:
                        pe.wait_ge(sem("merge_out"), f - 1)
                    else:
                        pe.wait_ge(sem("osb"), H)
                        pe.wait_ge(sem("fill_out"), 20)
                    if f == 0:
                        here(9)
                    if f % 4 == 0:
                        here(first)
                    wb = ring[:, 9 % RING2, :].rearrange("p (k n) -> p k n", k=4)
                    for k in range(4):
                        mm = pe.matmul(bank(b + 1), wb[:, k, f * P:(f + 1) * P], osb[:, k, :], start=k == 0, stop=k == 3)
                    mm.then_inc(sem("branch_mm" if f < KD - 1 else "blocks_used"), 1)
                else:
                    for k in range(4 * part - 4, 4 * part):
                        mm = pe.matmul(bank(b), place2(first)[:, k, f % 4 * P:(f % 4 + 1) * P], h3T[:, k, :], start=k == 0, stop=k == KD - 1)
                    if part == 2:
                        mm.then_inc(sem("merge_mm" if f % 4 < 3 else "blocks_used"), 1)

            def merge_at(*point):
                if point in MERGE_AT:
                    merge_piece(MERGE_AT[point])

            for n in range(2 * H):
                pe.wait_ge(sem("gsq"), n + 1)
                if n >= 3:
                    pe.wait_ge(sem("gexp"), n - 2)
                pe.matmul(bank(GSS[n % 3]), ONES, cu[:, n % 2, :], start=True, stop=True).then_inc(sem("gss_mm"), 1)
                merge_at("norm", n)
            pe.wait_ge(sem("gnormed"), 2 * H)
            for pair in range(H // 2):
                for p in range(2):
                    h = 2 * pair + p
                    if pair:
                        pe.wait_ge(sem("solve_dve"), SOLVE_DVE["w", h - 2])
                        pe.wait_ge(sem("u"), h - 1)
                    else:
                        pe.wait_ge(sem("colsab"), 2)
                    pe.matmul(bank(2 * p), IDENT[:, h:h + 1].to_broadcast([P, P]), rows, start=True, stop=True).then_inc(sem("solve_mm"), 1)
                    for q in range(NT):
                        t_ = slice(q * P, (q + 1) * P)
                        mm = pe.matmul(ps[:, 2 * p + 1, t_], gk[:, h, t_], gk[:, h, t_], start=True, stop=True)
                    mm.then_inc(sem("solve_mm"), 1)
                merge_at("solve", pair, 0)
                for p in range(2):
                    h = 2 * pair + p
                    pe.wait_ge(sem("solve_dve"), SOLVE_DVE["dec", h])
                    pe.wait_ge(sem("egrow"), h + 1)
                    pe.matmul(bank(2 * p), IDENT[:, 32 + h:33 + h].to_broadcast([P, P]), rows, start=True, stop=True).then_inc(sem("solve_mm"), 1)
                    pe.wait_ge(sem("solve_dve"), SOLVE_DVE["half", h])
                    for q in range(NT):
                        t_ = slice(q * P, (q + 1) * P)
                        mm = pe.matmul(ps[:, 2 * p + 1, t_], gk[:, h, t_], gq[:, h, t_], start=True, stop=True)
                    mm.then_inc(sem("solve_mm"), 1)
                merge_at("solve", pair, 1)
                for p in range(2):
                    h = 2 * pair + p
                    pe.wait_ge(sem("solve_dve"), SOLVE_DVE["mt", h])
                    for q in range(NT):
                        t_ = slice(q * P, (q + 1) * P)
                        mm = pe.transpose(ps[:, 2 * p, t_], gk[:, h, t_], IDENT)
                    mm.then_inc(sem("solve_mm"), 1)
                    pe.wait_ge(sem("solve_dve"), SOLVE_DVE["intra", h])
                    for q in range(NT):
                        t_ = slice(q * P, (q + 1) * P)
                        mm = pe.transpose(ps[:, 2 * p + 1, t_], gv[:, h, t_], IDENT)
                    mm.then_inc(sem("solve_mm"), 1)
                merge_at("solve", pair, 2)
                for p in range(2):
                    h = 2 * pair + p
                    pe.wait_ge(sem("solve_dve"), SOLVE_DVE["u0", h])
                    pe.wait_ge(sem("solve_dve"), SOLVE_DVE["kdec", h])
                    for q in range(NT):
                        mm = pe.transpose(ps[:, 2 * p, q * P:(q + 1) * P], Um[:, p, q, :], IDENT)
                    mm.then_inc(sem("solve_mm"), 1)
                merge_at("solve", pair, 3)
                for lv in range(1, 6):
                    for p in range(2):
                        h = 2 * pair + p
                        n = (5 * pair + lv - 1) * 2 + p
                        pe.wait_ge(sem("solve_dve"), SOLVE_DVE[("t0", h) if lv == 1 else ("t", h, lv - 1)])
                        pe.wait_ge(sem("mo"), n + 1)
                        if lv == 1:
                            pe.wait_ge(sem("solve_dve"), SOLVE_DVE["vrhs", h])
                        else:
                            pe.wait_ge(sem("solve_dve"), SOLVE_DVE["u", h, lv - 1])
                        for q in range(NT):
                            mm = pe.matmul(ps[:, 2 * p + 1, q * P:(q + 1) * P], Mo[:, p, q, :], Tm[:, p, q, :], start=True, stop=True)
                        mm.then_inc(sem("solve_mm"), 1)
                    for p in range(2):
                        n = (5 * pair + lv - 1) * 2 + p
                        pe.wait_ge(sem("yl"), n + 1)
                        if lv < 5:
                            for q in range(NT):
                                mm = pe.matmul(ps[:, 2 * p, q * P:(q + 1) * P], Um[:, p, q, :], Yl[:, p, q, :], start=True, stop=True)
                            mm.then_inc(sem("solve_mm"), 1)
                        for q in range(NT):
                            mm = pe.matmul(ps[:, 2 * p + 1, q * P:(q + 1) * P], Yl[:, p, q, :], Um[:, p, q, :], start=True, stop=True)
                        mm.then_inc(sem("solve_mm"), 1)
                for p in range(2):
                    h = 2 * pair + p
                    pe.wait_ge(sem("solve_dve"), SOLVE_DVE["u", h, 5])
                    for q in range(NT):
                        mm = pe.matmul(ps[:, 2 * p, q * P:(q + 1) * P], Um[:, p, q, :], rhs[:, p, q, 0:P], start=True, stop=True)
                    mm.then_inc(sem("solve_mm"), 1)
                    for q in range(NT):
                        mm = pe.matmul(ps[:, 2 * p + 1, q * P:(q + 1) * P], rhs[:, p, q, P:2 * P], Um[:, p, q, :], start=True, stop=True)
                    mm.then_inc(sem("solve_mm"), 1)
            pe.wait_ge(sem("cleared"), CLEARED["state"])
            pe.wait_ge(sem("u"), H)
            pe.wait_ge(sem("solve_dve"), SOLVE_DVE["w", H - 1])
            for c in range(S // CHUNK):
                q = c // 2
                vp = (vE, vO)[c % 2]
                if c:
                    pe.wait_ge(sem("chunk_new"), 5 * c)
                for h in range(H):
                    mm = pe.matmul(ps[:, 0, h * P:(h + 1) * P], wT[:, h, q, :], state[:, c % 2, h, :], start=True, stop=True)
                mm.then_inc(sem("chunk_mm"), 1)
                merge_at("chunk", c)
                if c >= 2:
                    pe.wait_ge(sem("og"), c - 1)
                pe.wait_ge(sem("chunk_new"), 5 * c + 1)
                for h in range(H):
                    mm = pe.matmul(ps[:, 1, h * P:(h + 1) * P], gk[:, h, q * P:(q + 1) * P], vp[:, h * P:(h + 1) * P], start=True, stop=True)
                mm.then_inc(sem("chunk_mm"), 1)
                for h in range(H):
                    pe.matmul(ps[:, 2 + c % 2, h * P:(h + 1) * P], gq[:, h, q * P:(q + 1) * P], state[:, c % 2, h, :], start=True, stop=False)
                    mm = pe.matmul(ps[:, 2 + c % 2, h * P:(h + 1) * P], intra[:, h, q, :], vp[:, h * P:(h + 1) * P], start=False, stop=True)
                mm.then_inc(sem("chunk_mm"), 1)
            for n in range(len(MERGE_AT), 3 * KD):
                merge_piece(n)

            def gate2(f):
                if f >= 4:
                    pe.wait_ge(sem("merge_out"), KD + f - 3)
                elif f >= 2:
                    pe.wait_ge(sem("merge_out"), KD + f - 3)
                else:
                    pe.wait_ge(sem("og"), 2 * NT)
                if f % 4 == 0:
                    here(11 + 2 * (f // 4))
                by_feature(place2(11 + 2 * (f // 4)), f % 4, 2 * (f % 4)).then_inc(sem("merge_mm" if f % 4 < 3 else "blocks_used"), 1)

            def branch2(f):
                wb = ring[:, 12 % RING2, :].rearrange("p (k n) -> p k n", k=4)
                for k in range(4):
                    mm = pe.matmul(bank(2 * (f % 4) + 1), wb[:, k, f * P:(f + 1) * P], ogT[:, k, :], start=k == 0, stop=k == 3)
                mm.then_inc(sem("branch_mm" if f < KD - 1 else "blocks_used"), 1)

            for f in range(4):
                gate2(f)
            pe.wait_ge(sem("ogated"), NT)
            for h in range(H):
                for q in range(NT):
                    mm = pe.transpose(ps[:, 2 * h + 1, q * P:(q + 1) * P], og[:, q, h * P:(h + 1) * P], IDENT)
                mm.then_inc(sem("og_turned"), 1)
            pe.wait_ge(sem("ogT"), H)
            here(12)
            for f in range(4):
                branch2(f)
            for f in range(4, KD):
                pe.wait_ge(sem("merge_out"), KD + f - 3)
                branch2(f)
                gate2(f)
            for m in (14, 15):
                here(m)
            pe.wait_ge(sem("merged"), KD)
            for q in range(NT):
                if q >= 2:
                    pe.wait_ge(sem("y_scaled"), q - 1)
                for n in range(2):
                    for k in range(KD):
                        mm = pe.matmul(bank(4 * (q % 2) + n), merged[:, k, q * P:(q + 1) * P], place2(14 + n)[:, k, :],
                                       start=k == 0, stop=k == KD - 1)
                mm.then_inc(sem("y2_mm"), 1)


        @block_.vector
        def _(dve):
            count = [0]

            def link(ins):
                count[0] += 1
                ins.then_inc(sem("dve_chain"), 1)
                dve.wait_ge(sem("dve_chain"), count[0])

            nc.vector.memset(modr, 0.0).then_inc(sem("vector_step"), 1)
            dve.wait_ge(sem("small_exp"), SMALL_EXP["c_exp"] + 1)
            link(nc.vector.tensor_scalar(cden, ce, 1.0, None, ALU.add))
            link(nc.vector.reciprocal(ce, cden))
            dve.wait_ge(sem("cleared"), CLEARED["cs"])
            dve.wait_ge(sem("c_in"), 32)
            nc.vector.tensor_tensor(cs[:, :, 0:2].rearrange("p k m -> p m k"), c2, ce.rearrange("p (m k) -> p m k", m=2), ALU.mult)\
                .then_inc(sem("vector_step"), 1)
            dve.wait_ge(sem("rms"), RMS["rstd"] + 1)
            for n in range(NT + NC):
                nc.vector.tensor_scalar(xc[:, n, :], xc[:, n, :], rstd[:, n:n + 1], None, ALU.mult).then_inc(sem("vector_step"), 1)
            dve.wait_ge(sem("broadcast"), BROADCAST["lambda"])
            for n in range(2):
                nc.vector.tensor_tensor_reduce(lamp[:, n, :], lamb[:, 2 * n, :], lamb[:, 2 * n + 1, :], 1.0, 0.0, ALU.mult, ALU.add,
                                               lams[:, n:n + 1]).then_inc(sem("vector_step"), 1)
            dve.wait_ge(sem("small_exp"), SMALL_EXP["lambda_exp"] + 1)
            link(nc.vector.tensor_tensor(lam, lame[:, 1:2], lame[:, 0:1], ALU.subtract))
            link(nc.vector.tensor_scalar(lam, lam, -LAMBDA_INIT, None, ALU.add))
            dve.wait_ge(sem("more_tables_in"), 48)
            link(nc.vector.tensor_scalar(gsub8, gsub, 1.0 - LAMBDA_INIT, None, ALU.mult))
            dve.wait_ge(sem("blocks_used"), 4)
            dve.wait_ge(sem("tables_in"), 144)
            nc.vector.tensor_tensor(modr[:, 0, :], bank(0), modr[:, 0, :], ALU.add).then_inc(sem("mod_rows"), 1)
            dve.wait_ge(sem("tensor_step"), TENSOR_STEP["mod_turned"] + 1)
            link(nc.vector.tensor_copy(modc.rearrange("p a b -> p (a b)"), bank(1)))
            for m in range(2):
                nc.vector.scalar_tensor_tensor(out=gain[:, m, :].rearrange("p (j q) -> p j q", j=2), in0=mhc[:, 2:4, :, m], scalar=1.0,
                                               in1=mhc[:, 0:2, :, 2], op0=ALU.add, op1=ALU.mult).then_inc(sem("vector_step"), 1)
            dve.wait_ge(sem("tensor_step"), TENSOR_STEP["wcs_mm"] + 1)
            for z in range(2):
                nc.vector.tensor_copy(wcs[:, :, z, :], bank(2 + z).rearrange("p (g d) -> p g d", g=H)).then_inc(sem("vector_step"), 1)
            dve.wait_ge(sem("vector_step"), VECTOR_STEP["gains"] + 2)
            for k in range(KD):
                dve.wait_ge(sem("x_turned"), k + 1)
                nc.vector.tensor_scalar(hT[:, k, :], bank(2 + k % 3), gain[:, 0, k:k + 1], mhc[:, k // 4, k % 4, 0:1],
                                        ALU.mult, ALU.add).then_inc(sem("hT"), 1)
            for g in range(H):
                if g < H - 1:
                    dve.wait_ge(sem("f_mm"), g + 1)
                else:
                    dve.wait_ge(sem("blocks_used"), B_F + 1)
                nc.vector.tensor_copy(fT[:, g, :], bank(g % 2)).then_inc(sem("fT"), 1)
            for g in range(H):
                dve.wait_ge(sem("mixf_mm"), g + 1)
                nc.vector.tensor_copy(mix_fou[:, g, :], bank(2 + g % 2)).then_inc(sem("mixf"), 1)
            for n in range(2 * H):
                dve.wait_ge(sem("qraw"), n + 1)
                dve.wait_ge(sem("more_tables_in"), 48)
                nc.vector.tensor_tensor(qcos, qraw[:, n % 2, :], rope[:, 0, :], ALU.mult).then_inc(sem("qcos"), 1)
                dve.wait_ge(sem("rotary_mm"), n + 1)
                link(nc.vector.tensor_tensor(bank(2 + n % 2), bank(2 + n % 2), rope[:, 1, :], ALU.mult))
                if n < H:
                    for m in range(2):
                        o = slice(HD * m, HD * (m + 1))
                        last = nc.vector.tensor_tensor(qz[o, n, m, :], ps[o, 2 + n % 2, :], qcos[o, :], ALU.add)
                        last.then_inc(sem("rotary_q"), 1)
                else:
                    last = nc.vector.tensor_tensor(kT[:, n - H, CTX:NKEY], bank(2 + n % 2), qcos, ALU.add)
                    last.then_inc(sem("rotary_q"), 1)
                dve.wait_ge(sem("rotary_q"), 2 * (n + 1) if n < H else 2 * H + n + 1 - H)
            for r in (1, 2):
                dve.wait_ge(sem("blocks_used"), B_ADA1 + 4 * r)
                nc.vector.tensor_tensor(modr[:, r, :], bank(5 + r), modr[:, r, :], ALU.add).then_inc(sem("mod_rows"), 1)

            def maxima(i):
                for m in range(2):
                    dve.wait_ge(sem("scores"), 2 * i + m + 1)
                    if i >= 1:
                        dve.wait_ge(sem("exps"), 2 * (i - 1) + m + 1)
                    nc.vector.tensor_reduce(nmax[:, m:m + 1], banks(2 * m, NKEY), AX.X, ALU.max, negate=True).then_inc(sem("score_max"), 1)

            def scales(i):
                dve.wait_ge(sem("exps"), 2 * i + 2)
                if i >= 1:
                    dve.wait_ge(sem("map1_scaled"), i)
                link(nc.vector.reciprocal(rz, zsum[:, 2 * (i % 2):2 * (i % 2) + 2]))
                nc.vector.tensor_tensor(rz[:, 1:2], rz[:, 1:2], lam, ALU.mult).then_inc(sem("pr_scales"), 1)

            def combine(i):
                dve.wait_ge(sem("map1_scaled"), i + 1)
                nc.vector.scalar_tensor_tensor(out=ex[:, i % 2, 0, :], in0=ex[:, i % 2, 0, :], scalar=rz[:, 0:1],
                                               in1=ex[:, i % 2, 1, :], op0=ALU.mult, op1=ALU.add).then_inc(sem("weights"), 1)
                dve.wait_ge(sem("weights"), i + 1)

            def norm_o(h):
                dve.wait_ge(sem("rms"), RMS["orstd"] + h + 1)
                if h >= 1:
                    dve.wait_ge(sem("o_turned"), h)
                for q in range(NT):
                    nc.vector.tensor_scalar(oz(q), ps[:, 6, q * P:(q + 1) * P], orstd[:, q:q + 1], None, ALU.mult)\
                        .then_inc(sem("o_normed"), 1)

            def mix_o(h):
                dve.wait_ge(sem("o_turned"), h + 1)
                nc.vector.tensor_scalar(mix_att[:, h, :], bank(7), gsub8, None, ALU.mult).then_inc(sem("mixa"), 1)

            maxima(0)
            maxima(1)
            for i in range(H * NT):
                scales(i)
                if i + 2 < H * NT:
                    maxima(i + 2)
                combine(i)
                if i % NT == 1 and i > NT:
                    norm_o(i // NT - 1)
                if i % NT == 3 and i > NT:
                    mix_o(i // NT - 1)
            norm_o(H - 1)
            mix_o(H - 1)

            dve.wait_ge(sem("broadcast"), BROADCAST["gt1"])
            dve.wait_ge(sem("x_again"), 16)
            for n in range(2):
                for q in range(NT):
                    if q < NT - 1:
                        dve.wait_ge(sem("y1_mm"), 3 * n + q + 1)
                    else:
                        dve.wait_ge(sem("blocks_used"), B_WOUT + n + 1)
                    half = slice(512 * n, 512 * n + 512)
                    link(nc.vector.tensor_tensor(bank(q), bank(q), gt1b[:, half], ALU.mult))
                    nc.vector.tensor_tensor(x1[:, q, half], x1[:, q, half], bank(q), ALU.add).then_inc(sem("x1_half"), 1)
            dve.wait_ge(sem("broadcast"), BROADCAST["ffn"])
            link(nc.vector.scalar_tensor_tensor(out=gsb, in0=gsb, scalar=1.0, in1=gffb, op0=ALU.add, op1=ALU.mult))
            for q in range(NT):
                dve.wait_ge(sem("rms"), RMS["rstd1"] + q + 1)
                link(nc.vector.scalar_tensor_tensor(out=h2[:, q, :], in0=x1[:, q, :], scalar=rstd[:, q:q + 1], in1=gsb,
                                                    op0=ALU.mult, op1=ALU.mult))
                nc.vector.tensor_tensor(h2[:, q, :], h2[:, q, :], sh2b, ALU.add).then_inc(sem("h2"), 1)

            def over(v, n):
                return v.unsqueeze(len(v.shape)).to_broadcast(list(v.shape) + [n])

            tt = nc.vector.tensor_tensor
            dve.wait_ge(sem("tensor_step"), TENSOR_STEP["logits_turned"] + 1)
            dve.wait_ge(sem("broadcast"), BROADCAST["rbias"])
            dve.wait_ge(sem("rcon_in"), 16)
            exp_no = rcon[:, 0:1, :].to_broadcast([P, NT, NEXP])
            grp_no = rcon[:, 1:2, 0:NGRP].to_broadcast([P, NT, NGRP])
            link(tt(L, ps[:, 7, 0:NT * 36].rearrange("p (q n) -> p q n", q=NT), rbias.unsqueeze(1).to_broadcast([P, NT, 36]), ALU.add))
            G, E_ = L[:, :, 0:NGRP], L[:, :, NGRP:36]
            link(nc.vector.tensor_reduce(gm, G, AX.X, ALU.max))
            tt(dg, G, over(gm, NGRP), ALU.subtract).then_inc(sem("router_diff"), 1)
            link(tt(ogr, G, over(gm, NGRP), ALU.is_equal))
            link(nc.vector.scalar_tensor_tensor(out=cg, in0=ogr, scalar=-99.0, in1=grp_no, op0=ALU.mult, op1=ALU.add))
            link(nc.vector.tensor_reduce(gi, cg, AX.X, ALU.min))
            link(tt(ogr, cg, over(gi, NGRP), ALU.is_equal))
            link(nc.vector.tensor_scalar(pen, ogr, -1.0, 1e30, ALU.add, ALU.mult))
            link(tt(Em.rearrange("p q (g e) -> p q g e", g=NGRP), E_.rearrange("p q (g e) -> p q g e", g=NGRP), over(pen, EPG), ALU.add))
            for O, m in ((O1, m1), (O2, m2)):
                link(nc.vector.tensor_reduce(m, Em, AX.X, ALU.max))
                link(tt(O, Em, over(m, NEXP), ALU.is_equal))
                link(nc.vector.scalar_tensor_tensor(out=Ec, in0=O, scalar=-99.0, in1=exp_no, op0=ALU.mult, op1=ALU.add))
                link(nc.vector.tensor_reduce(i1, Ec, AX.X, ALU.min))
                link(tt(O, Ec, over(i1, NEXP), ALU.is_equal))
                if O is O1:
                    link(nc.vector.scalar_tensor_tensor(out=Em, in0=O1, scalar=-3e30, in1=Em, op0=ALU.mult, op1=ALU.add))
            link(tt(As, O1, O2, ALU.add))
            link(nc.vector.memset(pre[:, 0, :], 0.0))
            for q in range(NT):
                link(tt(pre[:, q + 1, :], pre[:, q, :], As[:, q, :], ALU.add))
            nc.vector.memset(i2, 0.0).then_inc(sem("vector_step"), 1)
            dve.wait_ge(sem("small_exp"), SMALL_EXP["router_exp"] + 1)
            link(nc.vector.tensor_reduce(gs, dg, AX.X, ALU.add))
            link(nc.vector.reciprocal(pg, gs))
            tt(d2, m2, m1, ALU.subtract).then_inc(sem("router_diff"), 1)
            dve.wait_ge(sem("small_exp"), SMALL_EXP["router_exp"] + 2)
            link(nc.vector.tensor_scalar(den2, d2, 1.0, None, ALU.add))
            link(nc.vector.reciprocal(r2, den2))
            link(tt(wgt[:, 0, :], pg, r2, ALU.mult))
            link(tt(wgt[:, 1, :], wgt[:, 0, :], d2, ALU.mult))
            dve.wait_ge(sem("tensor_step"), TENSOR_STEP["ranks_mm"] + 1)
            link(nc.vector.tensor_copy(Rk, bank(0, P).rearrange("p (q e) -> p q e", q=NT)))
            for k, O in enumerate((O1, O2)):
                link(tt(tmpR, Rk, O, ALU.mult))
                link(nc.vector.tensor_reduce(rk[:, k, :], tmpR, AX.X, ALU.add))
                link(tt(tmpR, exp_no, O, ALU.mult))
                link(nc.vector.tensor_reduce(ek[:, k, :], tmpR, AX.X, ALU.add))
            link(nc.vector.tensor_copy(rki, rk.rearrange("p a b -> p (a b)")))
            link(nc.vector.tensor_copy(eki, ek.rearrange("p a b -> p (a b)")))
            link(nc.vector.tensor_scalar(lo, rki, CAP - 1, 8, ALU.bitwise_and, ALU.logical_shift_left))
            link(nc.vector.tensor_scalar(hi, rki, 6, 5, ALU.logical_shift_right, ALU.logical_shift_left))
            link(tt(lo, lo, hi, ALU.bitwise_or))
            link(nc.vector.tensor_copy(val, rcon[:, 2, 0:2 * NT]))
            link(nc.vector.reduce_max(flagf, bank(1, NEXP), AX.X))
            link(nc.vector.tensor_scalar(flagf, flagf, float(CAP), None, ALU.is_gt))
            nc.vector.tensor_copy(flag, flagf).then_inc(sem("vector_step"), 1)
            tt(slot, lo, eki, ALU.bitwise_or).then_inc(sem("vector_step"), 1)
            dve.wait_ge(sem("table_in"), 32)
            half = rcon[:, 3, 0:1].bitcast(I32).to_broadcast([P, ROUNDS * NEXP])
            link(nc.vector.tensor_scalar(tabs[:, 1, :], tabs[:, 0, :], -2, None, ALU.bitwise_and))
            link(tt(tabs[:, 1, :], tabs[:, 1, :], half, ALU.bitwise_or))
            link(nc.vector.tensor_scalar(tabs[:, 2, :], tabs[:, 0, :], 1, None, ALU.logical_shift_left))
            tt(tabs[:, 2, :], tabs[:, 2, :], half, ALU.bitwise_or).then_inc(sem("vector_step"), 1)

            def rows_out(u):
                nc.vector.tensor_copy(xeT[:, u, :, :].rearrange("p a b -> p (a b)"), bank(u)).then_inc(sem("xeT"), 1)

            def hidden(u, chain):
                nc.vector.tensor_scalar(ge[:, 1, :], ge[:, 0, :], 1.0, None, ALU.add).then_inc(sem("silu_steps"), 1)
                dve.wait_ge(sem("silu_steps"), chain + 1)
                nc.vector.reciprocal(ge[:, 2, :], ge[:, 1, :]).then_inc(sem("silu_steps"), 1)
                dve.wait_ge(sem("silu_steps"), chain + 2)
                nc.vector.tensor_tensor(ge[:, 3, :], ge[:, 2, :], bank(2, 256), ALU.mult).then_inc(sem("silu_steps"), 1)
                dve.wait_ge(sem("silu_steps"), chain + 3)

            def hidden_out(u):
                nc.vector.tensor_tensor(he[:, u, :], ge[:, 3, :], bank(3, 256), ALU.mult).then_inc(sem("hidden"), 1)

            def hidden_turned(u):
                nc.vector.tensor_copy(heT.rearrange("p a b -> p (a b)"), bank(4, 256)).then_inc(sem("heT"), 1)

            def result(u, signal):
                tt(ye[:, u, :], bank(6), gt2s, ALU.mult).then_inc(sem(signal), 1)

            for n in range(2):
                o = slice(64 * n, 64 * n + 64)
                link(nc.vector.tensor_copy(gt2s[o], gt2b[o, 512 * n:512 * n + 512]))
            dve.wait_ge(sem("xg_turned"), 1)
            rows_out(0)
            with dve.Fori(0, NEXP // 2) as i:
                for u in range(2):
                    dve.wait_ge(sem("gate_exp"), 2 * i + (u + 1))
                    hidden(u, 6 * i + 3 * u)
                    dve.wait_ge(sem("blocks_used"), 6 * i + (B_MOE + 3 * u + 2))
                    hidden_out(u)
                    dve.wait_ge(sem("xg_turned"), 2 * i + (u + 2))
                    rows_out(1 - u)
                    dve.wait_ge(sem("hidden_turned"), 2 * i + (u + 1))
                    hidden_turned(u)
                    dve.wait_ge(sem("blocks_used"), 6 * i + (B_MOE + 3 * u + 3))
                    dve.wait_ge(sem(f"ye_out_{u}"), 16 * i + 16)
                    result(u, "ye")
            more = dve.value_load(flag[0:1, 0:1], min_val=0, max_val=1)
            with dve.If(more > 0):
                with dve.Fori(0, (ROUNDS - 1) * NEXP) as n:
                    dve.wait_ge(sem("xg_turned"), n + (NEXP + 2))
                    rows_out(0)
                    dve.wait_ge(sem("gate_exp"), n + (NEXP + 1))
                    hidden(0, 3 * n + 3 * NEXP)
                    dve.wait_ge(sem("more_up"), n + 1)
                    hidden_out(0)
                    dve.wait_ge(sem("hidden_turned"), n + (NEXP + 1))
                    hidden_turned(0)
                    dve.wait_ge(sem("more_done"), n + 2)
                    result(0, "more_ye")
            def final_norm(q):
                dve.wait_ge(sem("rms"), RMS["rstd2"] + at_norm("final", q))
                nc.vector.scalar_tensor_tensor(out=x1[:, q, :], in0=x1[:, q, :], scalar=rstd[:, q:q + 1], in1=gfb,
                                               op0=ALU.mult, op1=ALU.mult).then_inc(sem("x3"), 1)

            def second_norm(q):
                dve.wait_ge(sem("rms"), RMS["rstd2"] + at_norm("second", q))
                nc.vector.tensor_scalar(h3[:, q, :], x1[:, q, :], rs3[:, q:q + 1], None, ALU.mult).then_inc(sem("h3"), 1)

            for q in range(NT):
                dve.wait_ge(sem(f"y_in_{q // 2}"), 32)
                y0, y1 = ygo[:, q, 0, :], ygo[:, q, 1, :]
                link(nc.vector.scalar_tensor_tensor(out=x1[:, q, :], in0=y0, scalar=wgt[:, 0, q:q + 1], in1=x1[:, q, :], op0=ALU.mult, op1=ALU.add))
                nc.vector.scalar_tensor_tensor(out=x1[:, q, :], in0=y1, scalar=wgt[:, 1, q:q + 1], in1=x1[:, q, :], op0=ALU.mult, op1=ALU.add)\
                    .then_inc(sem("x2"), 1)
                if q:
                    final_norm(q - 1)
                if q >= 2:
                    second_norm(q - 2)
            final_norm(NT - 1)
            second_norm(NT - 2)
            second_norm(NT - 1)

            dve.wait_ge(sem("tensor_step"), TENSOR_STEP["stage_turned"] + 1)
            nc.vector.tensor_copy(small[:, 200:256], ps[:, 7, 0:56]).then_inc(sem("vector_step"), 1)

            def dve_z(h):
                for n, kb in enumerate(reversed(range(NT))):
                    dve.wait_ge(sem("stick_ln"), 4 * h + n + 1)
                    nc.vector.scalar_tensor_tensor(out=spz[kb], in0=bank(kb, S - kb * P), scalar=0.0, in1=ezz[kb],
                                                   op0=ALU.max, op1=ALU.add).then_inc(sem("stick_sp"), 1)

            def silu_end(f):
                dve.wait_ge(sem("silu_exp"), f + 1)
                x_ = cv[:, f % 2, :]
                link(nc.vector.tensor_scalar(x_, x_, 1.0, None, ALU.add))
                link(nc.vector.reciprocal(x_, x_))
                if f < 4:
                    tt(osb[:, f, :], bank(5 + f % 3), x_, ALU.mult).then_inc(sem("fill_out"), 1)
                    dve.wait_ge(sem("fill_out"), f + 1)
                elif f >= 16:
                    tt(gg[:, f - 16, :], bank(5 + f % 3), x_, ALU.mult).then_inc(sem("fill_out"), 1)
                    dve.wait_ge(sem("fill_out"), f + 1)
                else:
                    g_ = gdn[f // 4 - 1][:, f % 4, :]
                    link(tt(g_, g_, x_, ALU.mult))
                nc.vector.memset(tick, 0.0).then_inc(sem("silu_done"), 1)
                dve.wait_ge(sem("silu_done"), f + 1)

            def dve_fill(f):
                if f:
                    silu_end(f - 1)
                if 4 <= f < 16:
                    if f % 4 == 3:
                        dve.wait_ge(sem("blocks_used"), B_SECOND + 3 + f // 4 + 1)
                    else:
                        dve.wait_ge(sem("fill_mm"), f + 1 - (f + 1) // 4)
                    g_, b_ = gdn[f // 4 - 1][:, f % 4, :], 5 + f % 3
                    ch = (4, 8, 0)[f // 4 - 1] + f % 4
                    link(nc.vector.tensor_scalar(g_, bank(b_), convw[:, 3, ch:ch + 1], None, ALU.mult))
                    for i in (2, 1, 0):
                        s_ = 3 - i
                        ins = nc.vector.scalar_tensor_tensor(out=g_[:, s_:S], in0=ps[:, b_, 0:S - s_], scalar=convw[:, i, ch:ch + 1],
                                                             in1=g_[:, s_:S], op0=ALU.mult, op1=ALU.add)
                        if i:
                            link(ins)
                    ins.then_inc(sem("fill_out"), 1)
                    dve.wait_ge(sem("fill_out"), f + 1)
                    nc.vector.memset(tick, 0.0).then_inc(sem("convolved"), 1)

            def dve_attend(h):
                if h % 2:
                    dve.wait_ge(sem("stick_o"), h + 1)
                    tt(osb[:, h // 2, :], osb[:, h // 2, :], bank(4), ALU.mult).then_inc(sem("osb"), 1)

            dve.wait_ge(sem("h3_turned"), KD)
            link(nc.vector.memset(trow, 0.0))
            nc.vector.memset(rows, 0.0).then_inc(sem("vector_step"), 1)
            link(nc.vector.memset(keep, 1.0))
            link(nc.vector.memset(keep.rearrange("p (c n) -> p c n", n=CHUNK)[:, :, 0:1], 0.0))
            dve.wait_ge(sem("tensor_step"), TENSOR_STEP["ab_mm"] + 1)
            dve.wait_ge(sem("columns_in"), 80)
            link(nc.vector.tensor_scalar(trow[0:4], ps[0:4, 0, :], dtb[0:4], None, ALU.add))
            nc.vector.scalar_tensor_tensor(out=trow2[0:4], in0=trow[0:4], scalar=-1.0, in1=trow[0:4], op0=ALU.mult, op1=ALU.max).then_inc(sem("vector_step"), 1)
            dve.wait_ge(sem("small_exp"), SMALL_EXP["dt_ln"] + 1)
            dve.wait_ge(sem("small_exp"), SMALL_EXP["alog_exp"] + 1)
            link(nc.vector.scalar_tensor_tensor(out=trow2[0:4], in0=trow[0:4], scalar=0.0, in1=trow2[0:4], op0=ALU.max, op1=ALU.add))
            link(nc.vector.tensor_scalar(trow2[0:4], trow2[0:4], nea[0:4], -1.0, ALU.mult, ALU.mult))
            nc.vector.tensor_tensor_scan(rows[0:4], keep[0:4], trow2[0:4], 0.0, ALU.mult, ALU.add).then_inc(sem("rows"), 1)
            dve.wait_ge(sem("rows"), 1)
            dve.wait_ge(sem("small_exp"), SMALL_EXP["beta_exp"] + 1)
            link(nc.vector.tensor_scalar(trow[32:36], trow[32:36], 1.0, None, ALU.add))
            nc.vector.reciprocal(rows[32:36], trow[32:36]).then_inc(sem("rows"), 1)
            chunked = rows[0:4].rearrange("p (c n) -> p c n", n=CHUNK)
            tt(trow[0:4].rearrange("p (c n) -> p c n", n=CHUNK), chunked[:, :, CHUNK - 1:CHUNK].to_broadcast([4, S // CHUNK, CHUNK]),
               chunked, ALU.subtract).then_inc(sem("vector_step"), 1)
            for what, n in STICK_PLAN:
                if what == "z":
                    dve_z(n)
                elif what == "fill":
                    dve_fill(n)
                elif what == "attend":
                    dve_attend(n)
            silu_end(19)

            def dve_merge(f):
                dve.wait_ge(sem("merge_exp"), f + 1)
                tt(merged[:, f, :], merged[:, f, :], bank(5 + 2 * (f % 2)), ALU.mult).then_inc(sem("merge_out"), 1)

            def merge_at(*point):
                if point in MERGE_AT and MERGE_AT[point] % 3 == 2:
                    dve_merge(MERGE_AT[point] // 3)

            dve.wait_ge(sem("tensor_step"), TENSOR_STEP["rows_turned"] + 1)
            nc.vector.tensor_copy(colsab, bank(1).rearrange("p (q c w) -> p q c w", q=NT, w=32)[:, :, 0:3, 0:H]).then_inc(sem("colsab"), 1)
            dve.wait_ge(sem("colsab"), 1)
            dve.wait_ge(sem("small_exp"), SMALL_EXP["egc"] + 1)
            tt(bg, egc, colsab[:, :, 1, :], ALU.mult).then_inc(sem("colsab"), 1)
            dve.wait_ge(sem("colsab"), 2)

            for n in range(2 * H):
                dve.wait_ge(sem("gexp"), n + 1)
                g_ = (gk, gq)[n // H][:, n % H, :]
                tt(g_, g_, cv[:, n % 2, :], ALU.mult).then_inc(sem("gnormed"), 1)
                merge_at("norm", n)
            def tiles(x):
                return x.rearrange("p (q n) -> p q n", q=NT)

            def by_row(x):
                return x.to_broadcast([P, NT, P])

            for pair in range(H // 2):
                for p in range(2):
                    h = 2 * pair + p
                    dve.wait_ge(sem("solve_mm"), SOLVE_MM["grow", h])
                    dve.wait_ge(sem("egrow"), h + 1)
                    for q in range(NT):
                        ins = nc.vector.tensor_scalar(dec[:, p, q, :], ps[:, 2 * p, q * P:(q + 1) * P], colsab[:, q, 0, h:h + 1], 0.0,
                                                      ALU.subtract, ALU.min)
                    ins.then_inc(sem("solve_dve"), 1)
                    nc.vector.tensor_copy(egl[:, h, :], egrow[:, p, CHUNK - 1:S:CHUNK]).then_inc(sem("solve_dve"), 1)
                    dve.wait_ge(sem("dec"), h + 1)
                    dve.wait_ge(sem("solve_mm"), SOLVE_MM["kk", h])
                    tt(MT[:, p, :, :], tiles(bank(2 * p + 1)), dec[:, p, :, :], ALU.mult).then_inc(sem("solve_dve"), 1)
                merge_at("solve", pair, 0)
                for p in range(2):
                    h = 2 * pair + p
                    dve.wait_ge(sem("solve_dve"), SOLVE_DVE["half", h])
                    dve.wait_ge(sem("solve_mm"), SOLVE_MM["brow", h])
                    tt(MT[:, p, :, :], MT[:, p, :, :], tiles(bank(2 * p)), ALU.mult).then_inc(sem("solve_dve"), 1)
                    dve.wait_ge(sem("solve_mm"), SOLVE_MM["qk", h])
                    tt(intra[:, h, :, :], tiles(bank(2 * p + 1)), dec[:, p, :, :], ALU.mult).then_inc(sem("solve_dve"), 1)
                    tt(gq[:, h, :], gq[:, h, :], egrow[:, p, :], ALU.mult).then_inc(sem("solve_dve"), 1)
                    dve.wait_ge(sem("solve_dve"), SOLVE_DVE["mt", h])
                    link(tt(Um[:, p, :, :], MT[:, p, :, :], JOIN[0].unsqueeze(1).to_broadcast([P, NT, P]), ALU.mult))
                    nc.vector.scalar_tensor_tensor(out=Um[:, p, :, :], in0=Um[:, p, :, :], scalar=-1.0,
                                                   in1=IDENT.unsqueeze(1).to_broadcast([P, NT, P]), op0=ALU.mult, op1=ALU.add).then_inc(sem("solve_dve"), 1)
                merge_at("solve", pair, 1)
                for p in range(2):
                    h = 2 * pair + p
                    dve.wait_ge(sem("solve_mm"), SOLVE_MM["k", h])
                    tt(rhs[:, p, :, P:2 * P], tiles(bank(2 * p)), by_row(bg[:, :, h:h + 1]), ALU.mult).then_inc(sem("solve_dve"), 1)
                    tt(tiles(gk[:, h, :]), tiles(bank(2 * p)), by_row(colsab[:, :, 2, h:h + 1]), ALU.mult).then_inc(sem("solve_dve"), 1)
                    dve.wait_ge(sem("solve_mm"), SOLVE_MM["v", h])
                    tt(rhs[:, p, :, 0:P], tiles(bank(2 * p + 1)), by_row(colsab[:, :, 1, h:h + 1]), ALU.mult).then_inc(sem("solve_dve"), 1)
                merge_at("solve", pair, 2)
                for p in range(2):
                    dve.wait_ge(sem("solve_mm"), SOLVE_MM["u0", 2 * pair + p])
                    nc.vector.tensor_copy(Tm[:, p, :, :], tiles(bank(2 * p))).then_inc(sem("solve_dve"), 1)
                merge_at("solve", pair, 3)
                for lv in range(1, 6):
                    for p in range(2):
                        h = 2 * pair + p
                        if lv < 5:
                            dve.wait_ge(sem("solve_dve"), SOLVE_DVE[("t0", h) if lv == 1 else ("t", h, lv - 1)])
                            dve.wait_ge(sem("solve_mm"), SOLVE_MM["t", h, lv])
                            tt(Tm[:, p, :, :], Tm[:, p, :, :], tiles(bank(2 * p)), ALU.subtract).then_inc(sem("solve_dve"), 1)
                        dve.wait_ge(sem("solve_mm"), SOLVE_MM["u", h, lv])
                        if lv > 1:
                            dve.wait_ge(sem("solve_dve"), SOLVE_DVE["u", h, lv - 1])
                        tt(Um[:, p, :, :], Um[:, p, :, :], tiles(bank(2 * p + 1)), ALU.subtract).then_inc(sem("solve_dve"), 1)
                for p in range(2):
                    h = 2 * pair + p
                    dve.wait_ge(sem("solve_mm"), SOLVE_MM["w", h])
                    nc.vector.tensor_copy(wT[:, h, :, :], tiles(bank(2 * p + 1))).then_inc(sem("solve_dve"), 1)
            def square_sums(q):
                dve.wait_ge(sem("og"), 2 * q + 2)
                link(tt(ogs, og[:, q, :], og[:, q, :], ALU.mult))
                nc.vector.tensor_reduce(oss2[:, 4 * q:4 * q + 4], ogs.rearrange("p (h n) -> p h n", h=H), AX.X, ALU.add).then_inc(sem("oss2"), 1)
                dve.wait_ge(sem("oss2"), q + 1)

            dve.wait_ge(sem("cleared"), CLEARED["state"])
            for c in range(S // CHUNK):
                o = slice(CHUNK * (c % 2), CHUNK * (c % 2) + CHUNK)
                vp = (vE, vO)[c % 2]
                dve.wait_ge(sem("chunk_mm"), 3 * c + 1)
                dve.wait_ge(sem("u"), H)
                tt(vp[o].rearrange("p (h n) -> p h n", h=H), gv[o].rearrange("p h (q n) -> p h q n", q=NT)[:, :, c // 2, :],
                   ps[o, 0, :].rearrange("p (h n) -> p h n", h=H), ALU.subtract).then_inc(sem("chunk_new"), 1)
                dve.wait_ge(sem("chunk_mm"), 3 * c + 2)
                if c:
                    dve.wait_ge(sem("chunk_new"), 5 * c)
                for h in range(H):
                    nc.vector.scalar_tensor_tensor(out=state[:, (c + 1) % 2, h, :], in0=state[:, c % 2, h, :], scalar=egl[:, h, c:c + 1],
                                                   in1=ps[:, 1, h * P:(h + 1) * P], op0=ALU.mult, op1=ALU.add).then_inc(sem("chunk_new"), 1)
                merge_at("chunk", c)
                if c % 2 and c >= 3:
                    square_sums((c - 3) // 2)
            dve_merge(KD - 2)
            dve_merge(KD - 1)
            square_sums(NT - 1)
            dve.wait_ge(sem("rms"), RMS["ors2"] + 1)
            for q in range(NT):
                link(tt(tiles(og[:, q, :]), tiles(og[:, q, :]), ors2[:, 4 * q:4 * q + 4].unsqueeze(2).to_broadcast([P, H, P]), ALU.mult))
                tt(og[:, q, :], og[:, q, :], gg[:, q, :], ALU.mult).then_inc(sem("ogated"), 1)
            for h in range(H):
                dve.wait_ge(sem("og_turned"), h + 1)
                nc.vector.tensor_scalar(ogT[:, h, :], bank(2 * h + 1), gnw, None, ALU.mult).then_inc(sem("ogT"), 1)
            for n in range(KD, 2 * KD):
                f = n % KD
                dve.wait_ge(sem("merge_exp"), n + 1)
                s0, s1 = sig[:, n % 2, 0, :], sig[:, n % 2, 1, :]
                link(nc.vector.tensor_scalar(s1, s0, 1.0, None, ALU.add))
                link(nc.vector.reciprocal(s1, s1))
                if f < KD - 1:
                    dve.wait_ge(sem("branch_mm"), n)
                else:
                    dve.wait_ge(sem("blocks_used"), B_SECOND + 13)
                tt(s1, s1, bank(2 * (f % 4) + 1), ALU.mult).then_inc(sem("merge_out"), 1)
                dve.wait_ge(sem("merge_out"), n + 1)
                tt(merged[:, f, :], merged[:, f, :], s1, ALU.add).then_inc(sem("merged"), 1)
            dve.wait_ge(sem("broadcast"), BROADCAST["postb"])
            for q in range(NT):
                dve.wait_ge(sem("rms"), RMS["frs"] + q + 1)
                nc.vector.scalar_tensor_tensor(out=yb[:, q, :], in0=banks(4 * (q % 2), D), scalar=frs[:, q:q + 1], in1=postb,
                                               op0=ALU.mult, op1=ALU.mult).then_inc(sem("y_scaled"), 1)
                dve.wait_ge(sem("y_scaled"), q + 1)
                tt(yb[:, q, :], yb[:, q, :], x1[:, q, :], ALU.add).then_inc(sem("out_ready"), 1)



def kernel(**inputs):
    import concourse.bacc as bacc
    from concourse.bass_utils import run_bass_kernel_spmd

    nc = bacc.Bacc("TRN2", target_bir_lowering=False, num_devices=1)
    arrays, a, t = {}, {}, {}
    tables = constants()
    del tables["names"]
    for held, views, prefix in ((inputs, a, "in_"), (tables, t, "table_")):
        for name, value in held.items():
            value = np.ascontiguousarray(value)
            arrays[prefix + name] = value
            views[name] = nc.dram_tensor(prefix + name, value.shape, F32, kind="ExternalInput").ap()
    out = nc.dram_tensor("out", (1, S, D), F32, kind="ExternalOutput").ap()
    scratch = {
        "h2": nc.dram_tensor("experts_inputs", (2 * S, D // 2), F32, kind="Internal").ap(),
        "y": nc.dram_tensor("experts_results", (4 * S, D // 2), F32, kind="Internal").ap(),
        "table": nc.dram_tensor("slots", (CAP * ROUNDS * NEXP, 1), U32, kind="Internal").ap(),
    }
    program(nc, a, t, out, scratch)
    r = run_bass_kernel_spmd(nc, [arrays], core_ids=[0])
    return r.results[0]["out"]
```
